# Optimizing a Trainium2 kernel written in Bass

```python
import jax, jax.numpy as jnp
from jax import lax
import numpy as np

D_MODEL = 1024
BATCH = 1
SEQ = 1024
DEPTH = 1

CHUNK = 64
QUERY_BLOCK = 128
FOX_HEAD_DIM = 64
N_FOX_HEADS = (D_MODEL // 2) // FOX_HEAD_DIM
D_FOX = N_FOX_HEADS * FOX_HEAD_DIM
GDN_HEAD_DIM = 128
N_GDN_HEADS = (D_MODEL // 2) // GDN_HEAD_DIM
D_GDN = N_GDN_HEADS * GDN_HEAD_DIM
D_MIX = D_FOX + D_GDN
CONV_K = 4
D_FF = 4 * D_MODEL
EPS = 1e-6
PROJ_SIZES = (D_FOX, D_FOX, D_FOX, N_FOX_HEADS, D_GDN, D_GDN, D_GDN, N_GDN_HEADS, N_GDN_HEADS, D_GDN)
D_PROJ = sum(PROJ_SIZES)

kernel_name = "fox_gdn_hymba_sandwich_block"

def rms_norm(x, w):
    xf = x.astype(jnp.float32)
    y = xf * lax.rsqrt(jnp.mean(xf * xf, axis=-1, keepdims=True) + EPS)
    return (y * w.astype(jnp.float32)).astype(x.dtype)

def causal_depthwise_conv(x, w):
    k, c = w.shape
    return lax.conv_general_dilated(
        x, w[:, None, :].astype(x.dtype), window_strides=(1,), padding=[(k - 1, 0)],
        dimension_numbers=("NWC", "WIO", "NWC"), feature_group_count=c)

def forgetting_attention(q, k, v, log_f):
    b, s, h, d = q.shape
    scale = d ** -0.5
    cum = jnp.cumsum(log_f, axis=1).transpose(0, 2, 1)
    outs = []
    for i in range(s // QUERY_BLOCK):
        qs, qe = i * QUERY_BLOCK, (i + 1) * QUERY_BLOCK
        qb = q[:, qs:qe]
        kb = k[:, :qe]
        vb = v[:, :qe]
        logits = jnp.einsum("bqhd,bkhd->bhqk", qb, kb).astype(jnp.float32) * scale
        logits = logits + cum[:, :, qs:qe, None] - cum[:, :, None, :qe]
        mask = jnp.arange(qe)[None, :] <= (qs + jnp.arange(QUERY_BLOCK))[:, None]
        logits = jnp.where(mask, logits, -jnp.inf)
        p = jax.nn.softmax(logits, axis=-1)
        outs.append(jnp.einsum("bhqk,bkhd->bqhd", p.astype(v.dtype), vb))
    return jnp.concatenate(outs, axis=1)

def gated_delta_chunked(q, k, v, g, beta):
    b, s, h, dk = q.shape
    dv = v.shape[-1]
    n = s // CHUNK

    def to_chunks(t):
        return t.reshape(b, n, CHUNK, h, t.shape[-1]).transpose(0, 3, 1, 2, 4)

    q, k, v = to_chunks(q), to_chunks(k), to_chunks(v)
    g = g.reshape(b, n, CHUNK, h).transpose(0, 3, 1, 2)
    beta = beta.reshape(b, n, CHUNK, h).transpose(0, 3, 1, 2)
    gc = jnp.cumsum(g, axis=-1)
    incl = jnp.tril(jnp.ones((CHUNK, CHUNK), dtype=bool))
    strict = jnp.tril(jnp.ones((CHUNK, CHUNK), dtype=bool), k=-1)
    decay = jnp.exp(jnp.where(incl, gc[..., :, None] - gc[..., None, :], -jnp.inf))
    k_beta = k * beta[..., None]
    v_beta = v * beta[..., None]
    m = jnp.where(strict, jnp.einsum("bhncd,bhnkd->bhnck", k_beta, k) * decay, 0.0)
    eye = jnp.broadcast_to(jnp.eye(CHUNK, dtype=m.dtype), m.shape)
    t_inv = lax.linalg.triangular_solve(eye + m, eye, left_side=True, lower=True,
                                        unit_diagonal=True)
    u = jnp.einsum("bhnck,bhnkv->bhncv", t_inv, v_beta)
    w = jnp.einsum("bhnck,bhnkd->bhncd", t_inv, k_beta * jnp.exp(gc)[..., None])
    a_intra = jnp.einsum("bhncd,bhnkd->bhnck", q, k) * decay
    q_dec = q * jnp.exp(gc)[..., None]
    k_dec = k * jnp.exp(gc[..., -1:] - gc)[..., None]
    g_last = jnp.exp(gc[..., -1])

    def step(state, inp):
        qd, kd, uc, wc, ac, gl = inp
        v_new = uc - jnp.einsum("bhcd,bhdv->bhcv", wc, state)
        o = jnp.einsum("bhcd,bhdv->bhcv", qd, state) + jnp.einsum("bhck,bhkv->bhcv", ac, v_new)
        state = state * gl[..., None, None] + jnp.einsum("bhcd,bhcv->bhdv", kd, v_new)
        return state, o

    def chunk_major(t):
        return jnp.moveaxis(t, 2, 0)

    state0 = jnp.zeros((b, h, dk, dv), dtype=jnp.float32)
    _, o = lax.scan(step, state0, (chunk_major(q_dec), chunk_major(k_dec), chunk_major(u),
                                   chunk_major(w), chunk_major(a_intra), chunk_major(g_last)))
    return o.transpose(1, 0, 3, 2, 4).reshape(b, s, h, dv)

def setup_inputs(seed: int = 0) -> dict:
    key = jax.random.key(seed)
    ks = jax.random.split(key, 16)
    f32 = jnp.float32

    def gain(k, n):
        return 1.0 + 0.1 * jax.random.normal(k, (n,), f32)

    x = jax.random.normal(ks[0], (BATCH, SEQ, D_MODEL), f32)
    pre_mix_norm = gain(ks[1], D_MODEL)
    w_in = jax.random.normal(ks[2], (D_MODEL, D_PROJ), f32) * D_MODEL ** -0.5
    fox_f_bias = 3.0 + 0.5 * jax.random.normal(ks[3], (N_FOX_HEADS,), f32)
    fox_out_norm = gain(ks[4], FOX_HEAD_DIM)
    gdn_conv_w = jax.random.normal(ks[5], (CONV_K, 3 * D_GDN), f32) * CONV_K ** -0.5
    gdn_a_log = jnp.log(jax.random.uniform(ks[6], (N_GDN_HEADS,), f32, 1.0, 16.0))
    dt = jnp.exp(jax.random.uniform(ks[7], (N_GDN_HEADS,), f32, np.log(1e-3), np.log(1e-1)))
    gdn_dt_bias = dt + jnp.log(-jnp.expm1(-dt))
    gdn_out_norm = gain(ks[8], GDN_HEAD_DIM)
    w_out = jax.random.normal(ks[9], (D_MIX, D_MODEL), f32) * D_MIX ** -0.5
    post_mix_norm = gain(ks[10], D_MODEL)
    pre_mlp_norm = gain(ks[11], D_MODEL)
    w_up = jax.random.normal(ks[12], (D_MODEL, D_FF), f32) * D_MODEL ** -0.5
    w_down = jax.random.normal(ks[13], (D_FF, D_MODEL), f32) * D_FF ** -0.5
    post_mlp_norm = gain(ks[14], D_MODEL)
    return {"x": x, "pre_mix_norm": pre_mix_norm, "w_in": w_in, "fox_f_bias": fox_f_bias,
            "fox_out_norm": fox_out_norm, "gdn_conv_w": gdn_conv_w, "gdn_a_log": gdn_a_log,
            "gdn_dt_bias": gdn_dt_bias, "gdn_out_norm": gdn_out_norm, "w_out": w_out,
            "post_mix_norm": post_mix_norm, "pre_mlp_norm": pre_mlp_norm, "w_up": w_up,
            "w_down": w_down, "post_mlp_norm": post_mlp_norm}

def reference(x, pre_mix_norm, w_in, fox_f_bias, fox_out_norm, gdn_conv_w, gdn_a_log,
              gdn_dt_bias, gdn_out_norm, w_out, post_mix_norm, pre_mlp_norm, w_up, w_down,
              post_mlp_norm):
    b, s, _ = x.shape
    split_at = [int(v) for v in np.cumsum(PROJ_SIZES)[:-1]]
    for _layer in range(DEPTH):
        h = rms_norm(x, pre_mix_norm)
        proj = h @ w_in
        fq, fk, fv, ff, gq, gk, gv, gb, ga, gz = jnp.split(proj, split_at, axis=-1)

        fq = fq.reshape(b, s, N_FOX_HEADS, FOX_HEAD_DIM)
        fk = fk.reshape(b, s, N_FOX_HEADS, FOX_HEAD_DIM)
        fv = fv.reshape(b, s, N_FOX_HEADS, FOX_HEAD_DIM)
        log_f = jax.nn.log_sigmoid(ff.astype(jnp.float32) + fox_f_bias.astype(jnp.float32))
        fox_o = forgetting_attention(fq, fk, fv, log_f)
        fox_o = rms_norm(fox_o, fox_out_norm).reshape(b, s, D_FOX)

        qkv = jax.nn.silu(causal_depthwise_conv(jnp.concatenate([gq, gk, gv], axis=-1), gdn_conv_w))
        qkv = qkv.astype(jnp.float32)
        cq, ck, cv = jnp.split(qkv, [D_GDN, 2 * D_GDN], axis=-1)
        cq = cq.reshape(b, s, N_GDN_HEADS, GDN_HEAD_DIM)
        ck = ck.reshape(b, s, N_GDN_HEADS, GDN_HEAD_DIM)
        cv = cv.reshape(b, s, N_GDN_HEADS, GDN_HEAD_DIM)
        cq = cq * lax.rsqrt(jnp.sum(cq * cq, axis=-1, keepdims=True) + EPS) * GDN_HEAD_DIM ** -0.5
        ck = ck * lax.rsqrt(jnp.sum(ck * ck, axis=-1, keepdims=True) + EPS)
        beta = jax.nn.sigmoid(gb.astype(jnp.float32))
        g = -jnp.exp(gdn_a_log.astype(jnp.float32)) * jax.nn.softplus(
            ga.astype(jnp.float32) + gdn_dt_bias.astype(jnp.float32))
        gdn_o = gated_delta_chunked(cq, ck, cv, g, beta)
        gate = jax.nn.silu(gz.astype(jnp.float32)).reshape(b, s, N_GDN_HEADS, GDN_HEAD_DIM)
        gdn_o = (rms_norm(gdn_o, gdn_out_norm) * gate).astype(x.dtype).reshape(b, s, D_GDN)

        mixed = jnp.concatenate([fox_o, gdn_o], axis=-1) @ w_out
        x = x + rms_norm(mixed, post_mix_norm)

        h = rms_norm(x, pre_mlp_norm)
        y = jnp.square(jax.nn.relu(h @ w_up)) @ w_down
        x = x + rms_norm(y, post_mlp_norm)
    return x


_drawn_inputs = setup_inputs


def setup_inputs(seed=0):
    import zlib

    import numpy as np

    out = dict(_drawn_inputs(seed))
    spreads = {}
    factors = {}
    for name, (base, spread) in spreads.items():
        noise = np.random.default_rng([zlib.crc32(name.encode()), seed]).standard_normal(out[name].shape)
        drawn = base * np.exp(spread * noise) if base else spread * noise
        out[name] = __import__('jax').numpy.asarray(drawn.astype(out[name].dtype))
    for name, factor in factors.items():
        out[name] = (out[name] * factor).astype(out[name].dtype)
    return out
```

```python
from contextlib import ExitStack

import concourse.bass as bass
from concourse import mybir

F32 = mybir.dt.float32
F32R = mybir.dt.float32r
BF16 = mybir.dt.bfloat16
ALU = mybir.AluOpType
ACT = mybir.ActivationFunctionType
AX_X = mybir.AxisListType.X

P = 128
SEQ = 1024
D = 1024
KT = D // P
NT = SEQ // P
HALF = SEQ // 2
D_FF = 4 * D
FT = D_FF // P
CHUNK = 64
NCHUNK = SEQ // CHUNK
FOX_HEADS, FOX_DIM = 8, 64
GDN_HEADS, GDN_DIM = 4, 128
D_GDN = GDN_HEADS * GDN_DIM
D_FOX = FOX_HEADS * FOX_DIM
TAPS = 4
EPS = 1e-6
LEVELS = 6
LOWEST = -3.0e38

FQ, FK, FV, FF = 0, D_FOX, 2 * D_FOX, 3 * D_FOX
GQ = FF + FOX_HEADS
GK, GV = GQ + D_GDN, GQ + 2 * D_GDN
GB = GQ + 3 * D_GDN
GA = GB + GDN_HEADS
GZ = GA + GDN_HEADS

BLOCKS = (FV, GZ, GQ, GK, GV, FQ, FK)
NB = len(BLOCKS)
CONV_BLOCKS = (2, 3, 4)
CQ, CK, CV, CZ = range(4)

ROW_CUM, ROW_BETA, ROW_G, ROW_REST = 0, 32, 64, 96
BETA, G_SUM, G_EXP, G_REST = range(4)

IDENT, DECAY_MASK, LEVEL_MASK = 0, 1, 2
N_CONST = 2 + LEVELS

PREP_FILLS = [
    ("gl", 0, 0), ("fv", 0, 0), ("fv", 1, 0), ("z", 0, 0), ("z", 1, 0),
    ("k", 0, 0), ("q", 0, 0), ("v", 0, 0), ("v", 1, 0), ("decay", 0, 0),
    ("knT", 0, 0), ("qnT", 0, 0),
    ("qdT", 0, 0), ("kbT", 0, 0), ("N", 0, 0), ("A", 0, 0), ("k", 1, 0), ("q", 1, 0),
    ("M0", 0, 0), ("knT", 1, 0), ("qnT", 1, 0), ("X", 0, 1),
    ("TX", 0, 1), ("XR", 0, 1), ("qdT", 1, 0), ("kbT", 1, 0), ("N", 1, 0), ("A", 1, 0),
    ("X", 0, 2),
    ("M0", 1, 0), ("TX", 0, 2), ("XR", 0, 2), ("X", 1, 1), ("X", 0, 3),
    ("TX", 1, 1), ("XR", 1, 1), ("TX", 0, 3), ("XR", 0, 3), ("X", 1, 2), ("X", 0, 4),
    ("TX", 1, 2), ("XR", 1, 2), ("TX", 0, 4), ("XR", 0, 4), ("X", 1, 3), ("X", 0, 5),
    ("TX", 1, 3), ("XR", 1, 3), ("XR", 0, 5), ("X", 1, 4), ("W", 0, 0), ("U", 0, 0),
    ("TX", 1, 4), ("XR", 1, 4), ("X", 1, 5), ("XR", 1, 5), ("W", 1, 0), ("U", 1, 0),
]
NFILL_BANKS = 6

PREP_UNITS = [(0, 10), (0, 11), (0, 12), (0, 13), (1, 0), (1, 1), (1, 2), (1, 3)]
SCAN_UNITS = [4, 5, 6, 7, 8, 9]
SCAN_STEP_PARTS = 3
OWN_STEPS = 4 * KT


def with_projection(fills):
    steps = len(PREP_UNITS) * KT
    out, step, due = [], 0, []

    def parts(count):
        nonlocal step
        for _ in range(count):
            out.append(("part", step, 0))
            unit, k = divmod(step, KT)
            if k == 0 and unit % 2 == 0 and unit + 2 < len(PREP_UNITS) + 1 and PREP_UNITS[unit][1] != 12:
                out.append(("split", unit + 2, 0))
            if k == KT - 1:
                due.append(("out", unit, 0))
                if PREP_UNITS[unit][1] == 13:
                    out.append(("split", unit + 1, 0))
            step += 1

    n, pause = 0, 0
    for fill in fills:
        out.append(fill)
        if fill[0] in ("gl", "decay"):
            continue
        n += 1
        while due:
            out.append(due.pop(0))
        if n == 2:
            parts(KT)
        elif n > 2:
            if step == OWN_STEPS and pause < 5:
                pause += 1
                continue
            left = len([f for f in fills if f[0] not in ("gl", "decay")]) - n + 1
            parts(1 if step < OWN_STEPS else max(1, (steps - step) // left))
    parts(steps - step)
    return out + due


PREP = with_projection(PREP_FILLS)


def numbered(names):
    return {name: n + 1 for n, name in enumerate(names)}


FILLS = [s for s in PREP_FILLS if s[0] not in ("gl", "decay")]
FILL = numbered(FILLS)
ACT_READS = ("fv", "z", "knT", "qnT", "qdT", "kbT", "X", "W")
DVE_READS = ("k", "q", "v", "N", "A", "M0", "TX", "XR", "U")

_act, _dve, _pool = [], [], []
for _s in PREP_FILLS:
    _w, _g, _l = _s
    if _w in ("k", "q"):
        _act.append(("square", _w, _g))
        _dve += [("mean", _w, _g), _s]
        _pool.append(("power", _w, _g))
    elif _w == "gl":
        _act.append(_s)
    elif _w == "decay":
        _pool += [("decay", 1), ("decay", 2)]
        _act.append(_s)
    elif _w in ACT_READS:
        _act.append(_s)
    elif _w in DVE_READS:
        _dve.append(_s)
    if _w == "knT":
        _pool += [("kd", _g), ("kb", _g), ("kbg", _g)]
    if _w == "qnT":
        _pool.append(("qd", _g))
    if _w == "N":
        _pool += [("level", _g, 0), ("R0", _g)]
    if _w == "M0":
        _pool.append(("level", _g, 1))
    if _w == "X" and _l < LEVELS - 1:
        _pool.append(("level", _g, _l + 1))
ACT_PREP, DVE_PREP, POOL_PREP = numbered(_act), numbered(_dve), numbered(_pool)
NFILL, NA, ND, NP_ = len(FILLS), len(_act), len(_dve), len(_pool)

FOX_TILES = [(hh, qb) for hh in range(2) for qb in range(NT)]
FOX_CHUNKS = [(i, c) for i, (_, qb) in enumerate(FOX_TILES) for c in range(qb // 4 + 1)]
FOX_CHUNK = {c: n for n, c in enumerate(FOX_CHUNKS)}
NFT, NFC = len(FOX_TILES), len(FOX_CHUNKS)
SCAN_OUTS = {(KT * n + KT - 1) // SCAN_STEP_PARTS: u for n, u in enumerate(SCAN_UNITS)}
SCAN_SPLITS = {1: 3, 6: 4, 11: 5}
W_OUT_STEPS = {2: 4, 4: 5, 9: 6, 11: 7}


def gemm_block(jn, b):
    return 1 + NB * jn + b


def slot_of(b):
    return b % 2


def block_before_in_slot(g, b):
    return g - 1 if b == 0 else g - 3 if b == 1 else g - 2


READS = 2 * (NB - 1)


def reads_done(jn, b, n):
    return (jn * READS + 2 * b) + (n + 3)


def loads_before(jn, b):
    return (4 * jn + b // 2 + 1) if b % 2 == 0 else (3 * jn + b // 2 + 1)


def wide(ap, n):
    return ap.unsqueeze(2).to_broadcast([ap.shape[0], ap.shape[1], n])


def stacked(ap, n):
    return ap.unsqueeze(1).to_broadcast([ap.shape[0], n, ap.shape[1]])


def build(nc, x, pre_mix_norm, w_in, fox_f_bias, fox_out_norm, gdn_conv_w, gdn_a_log,
          gdn_dt_bias, gdn_out_norm, w_out, post_mix_norm, pre_mlp_norm, w_up, w_down,
          post_mlp_norm, const_tiles, scan_keep, out, mixed, gate_dram):
    x = x.rearrange("a s d -> (a s) d")
    out = out.rearrange("a s d -> (a s) d")
    w_in_k = w_in.rearrange("(k p) n -> p k n", p=P)
    w_out_k = w_out.rearrange("(k p) n -> p k n", p=P)
    w_up_k = w_up.rearrange("(k p) n -> p k n", p=P)
    with ExitStack() as ctx:
        def sem(name):
            return ctx.enter_context(nc.semaphore(name))

        def held(scope, name, shape, dt=F32):
            return scope.enter_context(nc.sbuf_tensor(name, shape, dt))

        ps = ctx.enter_context(nc.psum_tensor("ps", [P, 8 * 512], F32))

        def banks(first, count=1):
            return ps[:, first * 512:(first + count) * 512]

        gemm_ps = banks(0, 2)
        scan_a, scan_b, fox_s, fox_t, fox_o = banks(2), banks(3), banks(4, 2), banks(6), banks(7)
        fill_banks = [banks(2), banks(3), banks(4), banks(5), banks(6), banks(7)]

        whole = ctx.enter_context(ExitStack())
        const = held(whole, "const", [P, N_CONST, P])
        big = ctx.enter_context(ExitStack())
        big_hi = big.enter_context(nc.sbuf_tensor("big_hi", [P, KT, SEQ], F32R, side="right"))
        big_lo = big.enter_context(nc.sbuf_tensor("big_lo", [P, KT, SEQ], F32R, side="right"))
        w_raw = [held(whole, f"w_raw{s}", [P, KT, P]) for s in range(2)]
        ident = const[:, IDENT, :]

        mix = ExitStack()
        w_hi = [held(mix, f"w_hi{s}", [P, KT, P], F32R) for s in range(2)]
        w_lo = [held(mix, f"w_lo{s}", [P, KT, P], F32R) for s in range(2)]
        q_fox = held(mix, "q_fox", [P, SEQ])
        k_split = [held(mix, f"k_split{hh}", [P, SEQ], F32R) for hh in range(2)]
        v_fox = held(mix, "v_fox", [P, SEQ])
        c_raw = held(mix, "c_raw", [P, 4, SEQ])
        taps_in = held(mix, "taps_in", [P, TAPS - 1 + HALF])
        zeros = held(mix, "zeros", [P, TAPS - 1])
        wait_holder = held(mix, "wait_holder", [P, 1])
        minus_half = held(mix, "minus_half", [P, 16])
        gates_all = held(mix, "gates_all", [P, 4, GDN_HEADS, NT])
        conv_all = held(mix, "conv_all", [P, TAPS * 3 * GDN_HEADS])
        fox_norm_row = held(mix, "fox_norm_row", [P, FOX_DIM])
        gdn_norm_row = held(mix, "gdn_norm_row", [P, GDN_DIM])
        taps = held(mix, "taps", [P, TAPS, 3])
        ident_bf = held(mix, "ident_bf", [P, P], BF16)
        causal_bf = held(mix, "causal_bf", [P, P], BF16)

        params_cleared = sem("params_cleared")
        params_loaded = sem("params_loaded")
        x_loaded = [sem(f"x_loaded{s}") for s in range(4)]
        gate_w_cleared = sem("gate_w_cleared")
        gate_w_loaded = sem("gate_w_loaded")
        w_loaded = [sem(f"w_loaded{s}") for s in range(2)]
        x_square = sem("x_square")
        x_mean = sem("x_mean")
        x_power = sem("x_power")
        x_normed = sem("x_normed")
        x_turned = sem("x_turned")
        x_hi = sem("x_hi")
        x_lo = sem("x_lo")
        w_hi_ready = sem("w_hi_ready")
        w_lo_ready = sem("w_lo_ready")
        gemm_done = sem("gemm_done")
        gemm_read = sem("gemm_read")
        gate_act = sem("gate_act")
        gate_dve = sem("gate_dve")
        gate_pool = sem("gate_pool")
        gate_turned = sem("gate_turned")
        stored = sem("stored")
        gates_ready = sem("gates_ready")
        taps_ready = sem("taps_ready")
        conv_step = sem("conv_step")
        silu_done = sem("silu_done")
        head_gates = sem("head_gates")
        head_taps = sem("head_taps")
        g_row_loaded = sem("g_row_loaded")
        cum_row_loaded = sem("cum_row_loaded")
        filled = sem("filled")
        act_prep = sem("act_prep")
        dve_prep = sem("dve_prep")
        pool_prep = sem("pool_prep")
        norm_sum = sem("norm_sum")
        half_ready = sem("half_ready")
        scan_v = sem("scan_v")
        scan_o = sem("scan_o")
        scan_s = sem("scan_s")
        v_new_ready = sem("v_new_ready")
        state_ready = sem("state_ready")
        o_read = sem("o_read")
        k_hi_ready = sem("k_hi_ready")
        k_lo_ready = sem("k_lo_ready")
        q_hi_ready = sem("q_hi_ready")
        q_ready = sem("q_ready")
        fox_scored = sem("fox_scored")
        fox_max = sem("fox_max")
        fox_neg_max = sem("fox_neg_max")
        fox_exp = sem("fox_exp")
        fox_turned = sem("fox_turned")
        pt_act = sem("pt_act")
        pt_dve = sem("pt_dve")
        fox_pv = sem("fox_pv")
        fox_inv = sem("fox_inv")
        fox_read = sem("fox_read")
        tail_square = sem("tail_square")
        tail_dve = sem("tail_dve")
        tail_power = sem("tail_power")
        mixed_ready = sem("mixed_ready")

        first = ExitStack()
        x_in = [held(first, f"x_in{s}", [P, D]) for s in range(4)]
        x_n = [held(first, f"x_n{s}", [P, D]) for s in range(2)]
        x_sq = held(first, "x_sq", [P, D])
        x_ss = held(first, "x_ss", [P, NT])
        x_ms = held(first, "x_ms", [P, NT])
        x_rs = held(first, "x_rs", [P, NT])
        pre_row = held(first, "pre_row", [P, D])
        causal = held(first, "causal", [P, P])
        keep = held(first, "keep", [P, SEQ])
        conv_rows = held(first, "conv_rows", [TAPS * 3 * GDN_HEADS, P])
        row_bias = held(first, "row_bias", [P, 1])
        row_a = held(first, "row_a", [P, 2])
        gate_y = held(first, "gate_y", [P, SEQ])
        gate_u = held(first, "gate_u", [P, SEQ])
        gate_e = held(first, "gate_e", [P, SEQ])
        gate_in = held(first, "gate_in", [P, SEQ])
        gate_rows = held(first, "gate_rows", [P, SEQ])
        first.close()

        cum_row = held(mix, "cum_row", [P, SEQ])
        decay = held(mix, "decay", [P, NT, P])
        v_tok = held(mix, "v_tok", [P, NT, P])
        z_tok = held(mix, "z_tok", [P, NT, P])
        kn = held(mix, "kn", [P, 4, P])
        qn = held(mix, "qn", [P, 4, P])
        kd = held(mix, "kd", [P, NT, P])
        kbg = held(mix, "kbg", [P, 2, 4, P])
        vb = held(mix, "vb", [P, 2, 4, P])
        knT = held(mix, "knT", [P, 4, P])
        qnT = held(mix, "qnT", [P, 4, P])
        kbT = held(mix, "kbT", [P, 4, P])
        qdT = held(mix, "qdT", [P, NT, P])
        n_low = held(mix, "n_low", [P, 2, 4, P])
        n_lev = held(mix, "n_lev", [P, 2, 4, P])
        t_inv = held(mix, "t_inv", [P, 2, 4, P])
        r_inv = held(mix, "r_inv", [P, 2, 4, P])
        xb = held(mix, "xb", [P, 2, 4, P])
        a_t = held(mix, "a_t", [P, NT, P])
        state = held(mix, "state", [P, P])
        v_new = held(mix, "v_new", [P, P])
        q_hi = [held(mix, f"q_hi{s}", [P, P], F32R) for s in range(2)]
        q_lo = [held(mix, f"q_lo{s}", [P, P], F32R) for s in range(2)]
        probs = [m.rearrange("p g t d -> p (g t d)") for m in (n_low[:, :, :, :], n_lev[:, :, :, :])]
        probs_t = [held(mix, f"probs_t{s}", [P, 4, P]) for s in range(2)]
        fox_out = held(mix, "fox_out", [P, NT, 2, FOX_DIM])
        g_head = held(mix, "g_head", [P, 4, NT])
        g_last = held(mix, "g_last", [P, NCHUNK])
        sums = held(mix, "sums", [P, 2, 4])
        means = held(mix, "means", [P, 2, 4])
        powers = held(mix, "powers", [P, 2, 4])
        row_max = held(mix, "row_max", [P, 2])
        neg_max = held(mix, "neg_max", [P, 2])
        row_sum = held(mix, "row_sum", [P, NFT])
        row_inv = held(mix, "row_inv", [P, NFT])
        tail_ss = held(mix, "tail_ss", [P, 16 + NT])
        tail_ms = held(mix, "tail_ms", [P, 16 + NT])
        tail_rs = tail_ms
        u_all = xb[:, :, :, :].rearrange("p g t d -> p (g t) d")
        w_all = t_inv[:, :, :, :].rearrange("p g t d -> p (g t) d")

        PARAM_LOADS = 10
        GATE_ROWS_DONE = 7

        def turned_gates(row):
            return banks(2, 2).rearrange("p (t r) -> p t r", r=P)[:, :, row:row + GDN_HEADS].rearrange("p t h -> p h t")

        def head_rows(hh):
            return slice(hh * FOX_DIM, (hh + 1) * FOX_DIM)

        def bank(f):
            return fill_banks[f % NFILL_BANKS]

        def bank4(f):
            return bank(f).rearrange("p (t d) -> p t d", t=4)

        def first_stage_over(eng):
            eng.wait_ge(x_lo, NT)
            eng.wait_ge(gates_ready, 5)
            eng.wait_ge(stored, 32)

        mix.close()
        late = ctx.enter_context(ExitStack())
        h2_hi = held(late, "h2_hi", [P, KT, SEQ], F32R)
        h2_lo = held(late, "h2_lo", [P, KT, SEQ], F32R)
        x_new = held(late, "x_new", [P, NT, D])
        halves = held(late, "halves", [P, 2])
        o_ss = held(late, "o_ss", [P, 3 * NT])
        o_ms = held(late, "o_ms", [P, 3 * NT])
        o_rs = held(late, "o_rs", [P, 3 * NT])
        late_d = ExitStack()
        post_mix_row = held(late_d, "post_mix_row", [P, D])
        pre_mlp_row = held(late_d, "pre_mlp_row", [P, D])
        m_hi = [held(late_d, f"m_hi{s}", [P, KT, P], F32R) for s in range(2)]
        m_lo = [held(late_d, f"m_lo{s}", [P, KT, P], F32R) for s in range(2)]
        y_buf = [held(late_d, f"y_buf{s}", [P, D]) for s in range(2)]
        late_d.close()
        big.close()
        post_mlp_row = held(late, "post_mlp_row", [P, D])
        act_ff = held(late, "act_ff", [P, FT, HALF])
        u_hi = [held(late, f"u_hi{s}", [P, KT, P], F32R) for s in range(2)]
        u_lo = [held(late, f"u_lo{s}", [P, KT, P], F32R) for s in range(2)]
        a_hi = [held(late, f"a_hi{s}", [P, HALF], F32R) for s in range(2)]
        a_lo = [held(late, f"a_lo{s}", [P, HALF], F32R) for s in range(2)]
        down_T = act_ff[:, FT - KT:FT, :]
        final = [act_ff[:, 16 + 2 * s:18 + 2 * s, :].rearrange("p a b -> p (a b)") for s in range(2)]
        final_sq = act_ff[:, 20:22, :].rearrange("p a b -> p (a b)")

        late_loaded = sem("late_loaded")
        m_turned = sem("m_turned")
        m_hi_ready = sem("m_hi_ready")
        m_lo_ready = sem("m_lo_ready")
        out_done = sem("out_done")
        o_square = sem("o_square")
        o_mean = sem("o_mean")
        o_power = sem("o_power")
        y_done = sem("y_done")
        x_new_ready = sem("x_new_ready")
        h2_normed = sem("h2_normed")
        h2_turned = sem("h2_turned")
        h2_hi_ready = sem("h2_hi_ready")
        h2_lo_ready = sem("h2_lo_ready")
        mlp_hi = sem("mlp_hi")
        mlp_lo = sem("mlp_lo")
        mlp_done = sem("mlp_done")
        relu_done = sem("relu_done")
        square_done = sem("square_done")
        act_hi = sem("act_hi")
        act_lo = sem("act_lo")
        down_act = sem("down_act")
        down_dve = sem("down_dve")
        final_turned = sem("final_turned")
        final_ready = sem("final_ready")
        final_step = sem("final_step")
        out_stored = [sem(f"out_stored{s}") for s in range(2)]
        HT = NT // 2
        STEPS = 2 * FT
        SLOT_LOADS = [loads_before(GDN_HEADS, KT - 2) + NT // 2, loads_before(GDN_HEADS, KT - 1) + NT // 2]
        W_OUT_SPLIT = gemm_block(GDN_HEADS, KT)

        def head_loop_over(eng):
            eng.wait_ge(stored, 32 + 32 * GDN_HEADS)

        def out_banks(t):
            return banks(2 * (t % 2), 2)

        def final_banks(tt):
            return banks(2 + 2 * (tt % 3), 2)

        block = ctx.enter_context(nc.Block())

        @block.sync
        def _(sp):
            for t in range(2):
                sp.dma_start(x_in[t][:, :], x[t * P:(t + 1) * P, :]).then_inc(x_loaded[t], 16)
            sp.dma_start(pre_row[:, :], pre_mix_norm.rearrange("(a d) -> a d", a=1).to_broadcast([P, D])).then_inc(params_loaded, 16)
            sp.dma_start(const[:, :, :], const_tiles[:, 0:N_CONST * P].rearrange("p (n m) -> p n m", m=P)).then_inc(params_loaded, 16)
            sp.dma_start(causal[:, :], const_tiles[:, N_CONST * P:(N_CONST + 1) * P]).then_inc(params_loaded, 16)
            for t in range(2, 4):
                sp.dma_start(x_in[t][:, :], x[t * P:(t + 1) * P, :]).then_inc(x_loaded[t], 16)
            sp.wait_ge(gate_w_cleared, 1)
            sp.dma_start(w_raw[0][:, :, ROW_CUM:ROW_CUM + FOX_HEADS], w_in_k[:, :, FF:FF + FOX_HEADS]).then_inc(gate_w_loaded, 16)
            sp.dma_start(w_raw[0][:, :, ROW_BETA:ROW_BETA + GDN_HEADS], w_in_k[:, :, GB:GB + GDN_HEADS]).then_inc(gate_w_loaded, 16)
            sp.dma_start(w_raw[0][:, :, ROW_G:ROW_G + GDN_HEADS], w_in_k[:, :, GA:GA + GDN_HEADS]).then_inc(gate_w_loaded, 16)
            sp.dma_start(keep[:, :], scan_keep).then_inc(params_loaded, 16)
            sp.wait_ge(params_cleared, 2)
            sp.dma_start(row_bias[ROW_CUM:ROW_CUM + FOX_HEADS, :], fox_f_bias.rearrange("(h a) -> h a", a=1)).then_inc(params_loaded, 16)
            sp.dma_start(row_bias[ROW_G:ROW_G + GDN_HEADS, :], gdn_dt_bias.rearrange("(h a) -> h a", a=1)).then_inc(params_loaded, 16)
            sp.dma_start(row_a[ROW_G:ROW_G + GDN_HEADS, 0:1], gdn_a_log.rearrange("(h a) -> h a", a=1)).then_inc(params_loaded, 16)
            sp.dma_start(conv_rows[:, :], gdn_conv_w.rearrange("t (b c) -> (t b) c", c=P)).then_inc(params_loaded, 16)
            sp.dma_start(fox_norm_row[:, :], fox_out_norm.rearrange("(a d) -> a d", a=1).to_broadcast([P, FOX_DIM])).then_inc(params_loaded, 16)
            sp.dma_start(gdn_norm_row[:, :], gdn_out_norm.rearrange("(a d) -> a d", a=1).to_broadcast([P, GDN_DIM])).then_inc(params_loaded, 16)

            def load_block(jn, b, first_col):
                g = gemm_block(jn, b)
                s = slot_of(b)
                before = block_before_in_slot(g, b)
                if not isinstance(before, int) or before >= 0:
                    sp.wait_ge(w_lo_ready, before + 1)
                sp.dma_start(w_raw[s][:, :, :], w_in_k[:, :, bass.ds(first_col + BLOCKS[b], P)]).then_inc(w_loaded[s], 16)

            load_block(0, 1, 0)
            for t in range(4, NT):
                sp.wait_ge(x_normed, t - 3)
                sp.dma_start(x_in[t % 4][:, :], x[t * P:(t + 1) * P, :]).then_inc(x_loaded[t % 4], 16)
            load_block(0, 0, 0)
            for b in range(2, NB):
                load_block(0, b, 0)
            sp.wait_ge(gate_dve, GATE_ROWS_DONE)
            sp.dma_start(gate_dram[0:FOX_HEADS, :], gate_rows[ROW_CUM:ROW_CUM + FOX_HEADS, :]).then_inc(stored, 16)
            sp.dma_start(gate_dram[FOX_HEADS:FOX_HEADS + GDN_HEADS, :], gate_rows[ROW_G:ROW_G + GDN_HEADS, :]).then_inc(stored, 16)
            sp.wait_ge(stored, 32)
            first_stage_over(sp)

            def head(j, with_gemm):
                looped = not isinstance(j, int)
                g_row = sp.snap(j + FOX_HEADS) if looped else j + FOX_HEADS
                cum_rows = [sp.snap(j * 2 + hh) if looped else j * 2 + hh for hh in range(2)]
                mixed_cols = [j * P + P + c for c in (0, D_FOX)]
                sp.wait_ge(dve_prep, j * ND + 1)
                sp.dma_start(decay[:, :, :].rearrange("p t d -> p (t d)"),
                             gate_dram[bass.ds(g_row, 1), :].to_broadcast([P, SEQ])).then_inc(g_row_loaded, 16)
                sp.wait_ge(fox_max, j * NFT + 1)
                sp.dma_start(cum_row[:, :], gate_dram[bass.ds(cum_rows[0], 1), :].to_broadcast([P, SEQ])).then_inc(cum_row_loaded, 16)
                def load_w_out(c):
                    g = gemm_block(j + 1, c)
                    sp.wait_ge(w_lo_ready, block_before_in_slot(g, c) + 1)
                    sp.dma_start(w_raw[slot_of(c)][:, :, :], w_out_k[:, :, c * P:(c + 1) * P]).then_inc(w_loaded[slot_of(c)], 16)

                for b in range(NB - 1 if with_gemm else KT - 2):
                    load_block(j + 1, b, j * P + P) if with_gemm else load_w_out(b)
                sp.wait_ge(fox_max, j * NFT + 1 + NT)
                sp.dma_start(cum_row[:, :], gate_dram[bass.ds(cum_rows[1], 1), :].to_broadcast([P, SEQ])).then_inc(cum_row_loaded, 16)
                if with_gemm:
                    load_block(j + 1, NB - 1, j * P + P)
                else:
                    for c in range(KT - 2, KT):
                        load_w_out(c)
                sp.wait_ge(mixed_ready, j * 2 + 1)
                sp.dma_start(mixed[:, bass.ds(mixed_cols[0], P)].rearrange("(t p) c -> p t c", p=P),
                             fox_out[:, :, :, :].rearrange("p t h d -> p t (h d)")).then_inc(stored, 16)
                sp.wait_ge(mixed_ready, j * 2 + 2)
                sp.dma_start(mixed[:, bass.ds(mixed_cols[1], P)].rearrange("(t p) c -> p t c", p=P),
                             u_all).then_inc(stored, 16)

            with sp.Fori(0, GDN_HEADS - 1) as j:
                head(j, True)
            head(GDN_HEADS - 1, False)
            head_loop_over(sp)
            for t in range(NT):
                if t >= 2:
                    sp.wait_ge(m_turned, t - 1)
                s = t % 2
                sp.dma_start(w_raw[s][:, :, :].rearrange("p k m -> p (k m)"), mixed[t * P:(t + 1) * P, P:P + D]).then_inc(w_loaded[s], 16)
                if t == 0:
                    sp.dma_start(post_mix_row[:, :], post_mix_norm.rearrange("(a d) -> a d", a=1).to_broadcast([P, D])).then_inc(late_loaded, 16)
                    sp.dma_start(x_new[:, :, :], x.rearrange("(t p) d -> p t d", p=P)).then_inc(late_loaded, 16)
                    sp.dma_start(pre_mlp_row[:, :], pre_mlp_norm.rearrange("(a d) -> a d", a=1).to_broadcast([P, D])).then_inc(late_loaded, 16)

            def load_up(h, f, s, wait):
                col = sp.snap(f * P) if not isinstance(f, int) else f * P
                if wait:
                    sp.wait_ge(mlp_lo, f + (h * STEPS - 1))
                sp.dma_start(w_raw[s][:, :, :], w_up_k[:, :, bass.ds(col, P)]).then_inc(w_loaded[s], 16)

            def load_down(h, f, s):
                row = sp.snap(f * P)
                sp.wait_ge(mlp_lo, f + (h * STEPS + FT - 1))
                sp.dma_start(w_raw[s][:, :, :].rearrange("p k m -> p (k m)"), w_down[bass.ds(row, P), :]).then_inc(w_loaded[s], 16)

            def store(h):
                for tt in range(HT):
                    t = h * HT + tt
                    sp.wait_ge(final_ready, t + 1)
                    sp.dma_start(out[t * P:(t + 1) * P, :], final[t % 2]).then_inc(out_stored[t % 2], 16)

            for h in range(2):
                if h == 0:
                    sp.wait_ge(m_turned, NT)
                load_up(h, 0, 0, h == 1)
                load_up(h, 1, 1, h == 1)
                if h == 0:
                    sp.wait_ge(h2_lo_ready, NT)
                    sp.dma_start(post_mlp_row[:, :], post_mlp_norm.rearrange("(a d) -> a d", a=1).to_broadcast([P, D])).then_inc(late_loaded, 16)
                if h == 1:
                    store(0)
                with sp.Fori(1, FT // 2) as i:
                    load_up(h, i * 2, 0, True)
                    load_up(h, i * 2 + 1, 1, True)
                with sp.Fori(0, FT // 2) as i:
                    load_down(h, i * 2, 0)
                    load_down(h, i * 2 + 1, 1)
            store(1)
            for s in range(2):
                sp.wait_ge(out_stored[s], 16 * NT // 2)

        @block.scalar
        def _(act):
            def unit(u, jn):
                b, n = u // 2, u % 2
                g = gemm_block(jn, b)
                act_out = slice(n * HALF, (n + 1) * HALF)
                src = gemm_ps[:, act_out]
                if b == NB - 1:
                    act.wait_ge(gemm_done, g * 2 + n + 1)
                    for hh in range(2):
                        hr = head_rows(hh)
                        nc.scalar.activation(k_split[hh][hr, act_out], src[hr, :], ACT.Copy).then_inc(k_hi_ready, 1)
                    return
                if u == 0 and (not isinstance(jn, int) or jn > 0):
                    act.wait_ge(k_lo_ready, jn * 4)
                if b in CONV_BLOCKS:
                    idx = 2 * CONV_BLOCKS.index(b) + n
                    if not isinstance(jn, int) or jn * 6 + idx > 0:
                        act.wait_ge(conv_step, (jn * 6 + idx) * TAPS)
                    act.wait_ge(gemm_done, g * 2 + n + 1)
                    halo = zeros[:, :] if n == 0 else taps_in[:, HALF:HALF + TAPS - 1]
                    nc.scalar.activation(taps_in[:, 0:TAPS - 1], halo, ACT.Copy).then_inc(taps_ready, 1)
                    act.wait_ge(taps_ready, jn * 6 + idx + 1)
                    nc.scalar.activation(taps_in[:, TAPS - 1:TAPS - 1 + HALF], src, ACT.Copy).then_inc(gemm_read, 1)
                else:
                    act.wait_ge(gemm_done, g * 2 + n + 1)
                    dst = {0: v_fox[:, act_out], 1: c_raw[:, CZ, act_out], 5: q_fox[:, act_out]}[b]
                    nc.scalar.activation(dst, src, ACT.Copy, scale=FOX_DIM ** -0.5 if b == 5 else 1.0).then_inc(gemm_read, 1)

            def split_hi(jn, b):
                g = gemm_block(jn, b)
                before = block_before_in_slot(g, b)
                act.wait_ge(w_loaded[slot_of(b)], loads_before(jn, b) * 16)
                if not isinstance(before, int) or before >= 0:
                    act.wait_ge(gemm_done, before * 2 + 2)
                nc.scalar.activation(w_hi[slot_of(b)][:, :, :], w_raw[slot_of(b)][:, :, :], ACT.Copy).then_inc(w_hi_ready, 1)

            def x_hi_part(t):
                act.wait_ge(x_turned, t + 1)
                nc.scalar.activation(big_hi[:, :, t * P:(t + 1) * P], banks(2 + 2 * (t % 2), 2).rearrange("p (k m) -> p k m", k=KT),
                                     ACT.Copy).then_inc(x_hi, 1)

            for t in range(NT):
                act.wait_ge(x_loaded[t % 4], 16 * (t // 4 + 1))
                if t >= 1:
                    act.wait_ge(x_square, t)
                nc.scalar.activation(x_sq[:, :], x_in[t % 4][:, :], ACT.Square, accum_out=x_ss[:, t:t + 1]).then_inc(x_square, 1)
                if t >= 1:
                    x_hi_part(t - 1)
            x_hi_part(NT - 1)
            act.wait_ge(gate_w_loaded, 48)
            nc.scalar.activation(w_hi[0][:, :, :], w_raw[0][:, :, :], ACT.Copy).then_inc(w_hi_ready, 1)
            split_hi(0, 0)
            act.wait_ge(params_loaded, PARAM_LOADS * 16)
            for n in range(2):
                act.wait_ge(gemm_done, n + 1)
                nc.scalar.activation(gate_y[:, n * HALF:(n + 1) * HALF], gemm_ps[:, n * HALF:(n + 1) * HALF], ACT.Identity,
                                     bias=row_bias[:, :]).then_inc(gemm_read, 1)
            act.wait_ge(gemm_read, 2)
            nc.scalar.activation(gate_u[:, :], gate_y[:, :], ACT.Abs).then_inc(gate_act, 1)
            act.wait_ge(gate_act, 1)
            nc.scalar.activation(gate_u[:, :], gate_u[:, :], ACT.Exp, scale=-1.0).then_inc(gate_act, 1)
            nc.scalar.activation(gate_e[ROW_BETA:ROW_BETA + 32, :], gate_y[ROW_BETA:ROW_BETA + 32, :], ACT.Exp, scale=-1.0).then_inc(gate_act, 1)
            nc.scalar.activation(row_a[:, 1:2], row_a[:, 0:1], ACT.Exp).then_inc(gate_act, 1)
            act.wait_ge(gate_act, 2)
            nc.scalar.activation(gate_u[:, :], gate_u[:, :], ACT.Ln, bias=1.0).then_inc(gate_act, 1)

            act.wait_ge(half_ready, 2)
            def split_and_unit(u, jn):
                if u % 2 == 0:
                    split_hi(jn, u // 2 + 1)
                unit(u, jn)

            for u in range(4):
                split_and_unit(u, 0)
            act.wait_ge(gates_ready, 3)
            for kind, row in ((G_EXP, ROW_G), (G_REST, ROW_REST)):
                nc.scalar.activation(gates_all[:, kind, :, :], turned_gates(row), ACT.Exp).then_inc(gates_ready, 1)
            for u in range(4, 10):
                split_and_unit(u, 0)

            def silu_all(jn):
                act.wait_ge(conv_step, jn * 6 * TAPS + 6 * TAPS)
                act.wait_ge(gemm_read, reads_done(jn, 1, 1))
                nc.scalar.activation(c_raw[:, :, :], c_raw[:, :, :], ACT.Silu).then_inc(silu_done, 1)

            silu_all(0)
            first_stage_over(act)

            def head(j, with_gemm):
                for step in PREP:
                    what, g, lev = step
                    if what in ("out", "split"):
                        ahead, u = PREP_UNITS[g] if g < len(PREP_UNITS) else (1, SCAN_UNITS[0])
                        if what == "out" and (with_gemm or not ahead):
                            unit(u, j + ahead)
                        elif what == "split" and (with_gemm or not ahead):
                            split_hi(j + ahead, u // 2)
                        elif what == "out":
                            w_out_hi(u)
                    elif what == "gl":
                        act.wait_ge(g_row_loaded, j * 16 + 16)
                        last = decay[:, :, :].rearrange("p t d -> p (t d)")[:, CHUNK - 1::CHUNK]
                        nc.scalar.activation(g_last[:, :], last, ACT.Exp).then_inc(act_prep, 1)
                    elif what == "decay":
                        act.wait_ge(pool_prep, j * NP_ + POOL_PREP[("decay", 2)])
                        nc.scalar.activation(decay[:, :, :], decay[:, :, :], ACT.Exp).then_inc(act_prep, 1)
                    elif what in ("k", "q"):
                        act.wait_ge(filled, j * NFILL + FILL[step])
                        if what == "k" and g == 1:
                            act.wait_ge(pool_prep, j * NP_ + POOL_PREP[("kbg", 0)])
                        dst = kn if what == "k" else qn
                        nc.scalar.activation(dst[:, :, :], bank4(FILL[step] - 1), ACT.Square).then_inc(act_prep, 1)
                    elif what in ACT_READS:
                        dst = {"fv": v_tok[:, 4 * g:4 * g + 4, :], "z": z_tok[:, 4 * g:4 * g + 4, :],
                               "knT": knT[:, :, :], "qnT": qnT[:, :, :], "kbT": kbT[:, :, :],
                               "qdT": qdT[:, 4 * g:4 * g + 4, :], "X": xb[:, g, :, :], "W": t_inv[:, g, :, :]}[what]
                        act.wait_ge(filled, j * NFILL + FILL[step])
                        if what == "X" and lev == 1:
                            act.wait_ge(stored, j * 32 + 32)
                        nc.scalar.activation(dst, bank4(FILL[step] - 1), ACT.Copy).then_inc(act_prep, 1)

                def p_chunk(i, c):
                    n = FOX_CHUNK[(i, c)]
                    if n % 2 == 1:
                        return
                    nb = min(4, FOX_TILES[i][1] + 1 - 4 * c)
                    act.wait_ge(fox_turned, j * NFC + n + 1)
                    if n >= 2:
                        act.wait_ge(fox_pv, j * NFC + n - 1)
                    nc.scalar.activation(probs_t[0][:, 0:nb, :], fox_t[:, 0:nb * P].rearrange("p (t d) -> p t d", t=nb),
                                         ACT.Copy).then_inc(pt_act, 1)

                def queries_hi(i):
                    hh, qb = FOX_TILES[i]
                    if i >= 2:
                        act.wait_ge(fox_scored, j * NFT + i - 1)
                    for rows in (head_rows(hh), head_rows(1 - hh)):
                        nc.scalar.activation(q_hi[i % 2][rows, :], q_fox[head_rows(hh), qb * P:(qb + 1) * P], ACT.Copy).then_inc(q_hi_ready, 1)

                queries_hi(0)
                for i in range(NCHUNK + 1):
                    if i + 1 < NCHUNK:
                        queries_hi(i + 1)
                    if i >= 1:
                        p_chunk(i - 1, 0)
                    if i < NCHUNK:
                        nk = (FOX_TILES[i][1] + 1) * P
                        act.wait_ge(fox_neg_max, j * NFT + i + 1)
                        nc.scalar.activation(probs[i % 2][:, 0:nk], probs[i % 2][:, 0:nk], ACT.Exp, bias=neg_max[:, i % 2:i % 2 + 1],
                                             accum_out=row_sum[:, i:i + 1]).then_inc(fox_exp, 1)
                        rows, (g, tt) = slice(64 * (i % 2), 64 * (i % 2) + 64), divmod(i // 2, 4)
                        act.wait_ge(scan_o, j * NCHUNK + i + 1)
                        nc.scalar.activation(xb[rows, g, tt, :], scan_b[rows, 0:P], ACT.Copy).then_inc(o_read, 1)
                    if i >= 1 and FOX_TILES[i - 1][1] >= 4:
                        p_chunk(i - 1, 1)
                    if with_gemm and i in SCAN_SPLITS:
                        split_hi(j + 1, SCAN_SPLITS[i])
                    if with_gemm and i in SCAN_OUTS:
                        unit(SCAN_OUTS[i], j + 1)
                    if not with_gemm and i in W_OUT_STEPS:
                        w_out_hi(W_OUT_STEPS[i])
                act.wait_ge(fox_read, j * NFT + NFT + 1)
                nc.scalar.activation(probs[0][:, :], fox_out[:, :, :, :].rearrange("p t h d -> p (t h d)"), ACT.Square).then_inc(tail_square, 1)
                act.wait_ge(o_read, j * NCHUNK + NCHUNK)
                nc.scalar.activation(probs[1][:, :], u_all.rearrange("p t d -> p (t d)"), ACT.Square).then_inc(tail_square, 1)
                if with_gemm:
                    silu_all(j + 1)

            def w_out_hi(c):
                g = gemm_block(GDN_HEADS, c)
                act.wait_ge(w_loaded[slot_of(c)], loads_before(GDN_HEADS, c) * 16)
                act.wait_ge(gemm_done, 2 * gemm_block(GDN_HEADS, 0))
                nc.scalar.activation(big_hi[:, :, c * P:(c + 1) * P], w_raw[slot_of(c)][:, :, :], ACT.Copy).then_inc(w_hi_ready, 1)

            with act.Fori(0, GDN_HEADS - 1) as j:
                head(j, True)
            head(GDN_HEADS - 1, False)
            head_loop_over(act)

            def m_hi_part(t):
                act.wait_ge(m_turned, t + 1)
                if t >= 2:
                    act.wait_ge(out_done, t - 1)
                nc.scalar.activation(m_hi[t % 2][:, :, :], fox_s.rearrange("p (k m) -> p k m", k=KT), ACT.Copy).then_inc(m_hi_ready, 1)

            def h2_hi_part(t):
                act.wait_ge(h2_turned, t + 1)
                nc.scalar.activation(h2_hi[:, :, t * P:(t + 1) * P], banks(6, 2).rearrange("p (k m) -> p k m", k=KT), ACT.Copy).then_inc(h2_hi_ready, 1)

            m_hi_part(0)
            for t in range(NT):
                if t + 1 < NT:
                    m_hi_part(t + 1)
                act.wait_ge(out_done, t + 1)
                if t >= 2:
                    act.wait_ge(h2_turned, t - 1)
                nc.scalar.activation(y_buf[t % 2][:, :], out_banks(t), ACT.Square, accum_out=o_ss[:, t:t + 1]).then_inc(o_square, 1)
                if t >= 1:
                    h2_hi_part(t - 1)
                act.wait_ge(x_new_ready, t + 1)
                nc.scalar.activation(y_buf[t % 2][:, :], x_new[:, t, :], ACT.Square, accum_out=o_ss[:, NT + t:NT + t + 1]).then_inc(o_square, 1)
            h2_hi_part(NT - 1)
            act.wait_ge(h2_lo_ready, NT)

            def up_hi(h, f, s):
                act.wait_ge(w_loaded[s], f * 8 + 16 * (h * STEPS // 2 + SLOT_LOADS[s] + 1) - 8 * s)
                if not isinstance(f, int) or h * STEPS + f >= 2:
                    act.wait_ge(mlp_done, f + (h * STEPS - 1))
                nc.scalar.activation(u_hi[s][:, :, :], w_raw[s][:, :, :], ACT.Copy).then_inc(mlp_hi, 1)

            def relu(h, f, s):
                act.wait_ge(mlp_done, f + (h * STEPS + 1))
                nc.scalar.activation(act_ff[:, bass.ds(f, 1), :].rearrange("p a t -> p (a t)"), banks(s), ACT.Relu).then_inc(relu_done, 1)

            def down_hi(h, f, s):
                up_hi(h, f + FT, s)
                act.wait_ge(square_done, f + (h * FT + 1))
                nc.scalar.activation(a_hi[s][:, :], act_ff[:, bass.ds(f, 1), :].rearrange("p a t -> p (a t)"), ACT.Copy).then_inc(act_hi, 1)

            def out_of_down(h):
                act.wait_ge(mlp_done, (h + 1) * STEPS)
                for m in range(0, KT, 2):
                    nc.scalar.activation(down_T[:, m, :], banks(m), ACT.Copy).then_inc(down_act, 1)

            def final_square(h, tts):
                for tt in tts:
                    t = h * HT + tt
                    act.wait_ge(final_turned, t + 1)
                    act.wait_ge(o_square, 2 * NT + t)
                    nc.scalar.activation(final_sq, final_banks(tt), ACT.Square, accum_out=o_ss[:, 2 * NT + t:2 * NT + t + 1]).then_inc(o_square, 1)

            for h in range(2):
                up_hi(h, 0, 0)
                up_hi(h, 1, 1)
                relu(h, 0, 0)
                if h == 1:
                    final_square(0, range(0, 2))
                    final_square(0, range(2, HT))
                    for s in range(2):
                        act.wait_ge(out_stored[s], 16 * HT // 2)
                with act.Fori(1, FT // 2) as i:
                    up_hi(h, i * 2, 0)
                    relu(h, i * 2 - 1, 1)
                    up_hi(h, i * 2 + 1, 1)
                    relu(h, i * 2, 0)
                relu(h, FT - 1, 1)
                with act.Fori(0, FT // 2) as i:
                    down_hi(h, i * 2, 0)
                    down_hi(h, i * 2 + 1, 1)
                out_of_down(h)
            final_square(1, range(HT))

        @block.vector
        def _(dve):
            def split_lo(jn, b):
                g = gemm_block(jn, b)
                dve.wait_ge(w_hi_ready, g + 1)
                dve.wait_ge(w_lo_ready, g)
                nc.vector.tensor_tensor(w_lo[slot_of(b)][:, :, :], w_raw[slot_of(b)][:, :, :], w_hi[slot_of(b)][:, :, :].bitcast(F32),
                                        ALU.subtract).then_inc(w_lo_ready, 1)

            def head_taps_copy(jn):
                src = conv_all[:, :].rearrange("p (t k h) -> p t k h", t=TAPS, k=3)[:, :, :, bass.ds(jn, 1)]
                nc.vector.tensor_copy(taps[:, :, :], src.rearrange("p t k h -> p t (k h)")).then_inc(head_taps, 1)

            def unit(u, jn, first_tap=0, last_tap=TAPS - 1):
                b, n = u // 2, u % 2
                if b == NB - 1:
                    cols = slice(n * HALF, (n + 1) * HALF)
                    for hh in range(2):
                        hr, other = head_rows(hh), head_rows(1 - hh)
                        dve.wait_ge(k_hi_ready, (jn * 4 + 2 * n) + hh + 1)
                        step = nc.vector.tensor_tensor(k_split[hh][other, cols], gemm_ps[hr, cols], k_split[hh][hr, cols].bitcast(F32), ALU.subtract)
                        step.then_inc(k_lo_ready, 1)
                    return
                if b not in CONV_BLOCKS:
                    return
                kind = CONV_BLOCKS.index(b)
                done = (jn * 6 + 2 * kind + n) * TAPS
                dst = c_raw[:, kind, n * HALF:(n + 1) * HALF]
                if first_tap == 0:
                    if kind == 0 and n == 0:
                        dve.wait_ge(head_taps, jn + 1)
                    dve.wait_ge(gemm_read, reads_done(jn, b, n))
                    nc.vector.tensor_scalar(dst, taps_in[:, 0:HALF], taps[:, 0, kind:kind + 1], None, ALU.mult).then_inc(conv_step, 1)
                for tap in range(max(first_tap, 1), last_tap + 1):
                    dve.wait_ge(conv_step, done + tap)
                    nc.vector.scalar_tensor_tensor(out=dst, in0=taps_in[:, tap:tap + HALF], scalar=taps[:, tap, kind:kind + 1],
                                                   in1=dst, op0=ALU.mult, op1=ALU.add).then_inc(conv_step, 1)

            def x_lo_part(t):
                dve.wait_ge(x_hi, t + 1)
                cols = slice(t * P, (t + 1) * P)
                nc.vector.tensor_tensor(big_lo[:, :, cols], banks(2 + 2 * (t % 2), 2).rearrange("p (k m) -> p k m", k=KT),
                                        big_hi[:, :, cols].bitcast(F32), ALU.subtract).then_inc(x_lo, 1)

            for t in range(NT):
                dve.wait_ge(x_square, t + 1)
                nc.vector.tensor_scalar(x_ms[:, t:t + 1], x_ss[:, t:t + 1], 1.0 / D, EPS, ALU.mult, ALU.add).then_inc(x_mean, 1)
                if t >= 1:
                    x_lo_part(t - 1)
                if t == 0:
                    dve.wait_ge(params_loaded, PARAM_LOADS * 16)
                if t >= 2:
                    dve.wait_ge(x_turned, t - 1)
                dve.wait_ge(x_power, t + 1)
                nc.vector.scalar_tensor_tensor(out=x_n[t % 2][:, :], in0=x_in[t % 4][:, :], scalar=x_rs[:, t:t + 1], in1=pre_row[:, :],
                                               op0=ALU.mult, op1=ALU.mult).then_inc(x_normed, 1)
            x_lo_part(NT - 1)
            dve.wait_ge(w_hi_ready, 1)
            nc.vector.tensor_tensor(w_lo[0][:, :, :], w_raw[0][:, :, :], w_hi[0][:, :, :].bitcast(F32), ALU.subtract).then_inc(w_lo_ready, 1)
            split_lo(0, 0)
            nc.vector.tensor_copy(ident_bf[:, :], ident).then_inc(dve_prep, 1)
            nc.vector.tensor_copy(causal_bf[:, :], causal[:, :]).then_inc(fox_max, 1)
            nc.vector.memset(taps_in[:, 0:TAPS - 1], 0.0).then_inc(fox_read, 1)
            fox_rows = slice(ROW_CUM, ROW_CUM + FOX_HEADS)
            g_rows = slice(ROW_G, ROW_G + GDN_HEADS)
            b_rows = slice(ROW_BETA, ROW_BETA + GDN_HEADS)
            r_rows = slice(ROW_REST, ROW_REST + GDN_HEADS)
            dve.wait_ge(gate_act, 5)
            dve.wait_ge(gate_pool, 1)
            nc.vector.scalar_tensor_tensor(out=gate_in[fox_rows, :], in0=gate_y[fox_rows, :], scalar=0.0, in1=gate_u[fox_rows, :],
                                           op0=ALU.min, op1=ALU.subtract, reverse1=True).then_inc(gate_dve, 1)
            nc.vector.scalar_tensor_tensor(out=gate_in[g_rows, :], in0=gate_y[g_rows, :], scalar=0.0, in1=gate_u[g_rows, :],
                                           op0=ALU.max, op1=ALU.add).then_inc(gate_dve, 1)
            dve.wait_ge(gate_dve, 2)
            nc.vector.tensor_scalar(gate_in[g_rows, :], gate_in[g_rows, :], row_a[g_rows, 1:2], -1.0, ALU.mult, ALU.mult).then_inc(gate_dve, 1)
            dve.wait_ge(gate_dve, 3)
            nc.vector.tensor_tensor_scan(gate_rows[:, :], keep[:, :], gate_in[:, :], 0.0, ALU.mult, ALU.add).then_inc(gate_dve, 1)
            nc.vector.tensor_scalar(gate_e[b_rows, :], gate_e[b_rows, :], 1.0, None, ALU.add).then_inc(gate_dve, 1)
            dve.wait_ge(gate_dve, 5)
            nc.vector.reciprocal(gate_rows[b_rows, :], gate_e[b_rows, :]).then_inc(gate_dve, 1)
            by_chunk = gate_rows[g_rows, :].rearrange("p (n c) -> p n c", c=CHUNK)
            nc.vector.tensor_tensor(gate_rows[r_rows, :].rearrange("p (n c) -> p n c", c=CHUNK),
                                    by_chunk[:, :, CHUNK - 1:CHUNK].to_broadcast([GDN_HEADS, NCHUNK, CHUNK]), by_chunk,
                                    ALU.subtract).then_inc(gate_dve, 1)
            dve.wait_ge(gate_turned, 1)
            nc.vector.tensor_copy(conv_all[:, :], fox_t[:, 0:TAPS * 3 * GDN_HEADS]).then_inc(gates_ready, 1)
            dve.wait_ge(gates_ready, 1)
            head_taps_copy(0)
            def split_and_unit(u, jn):
                if u % 2 == 0:
                    split_lo(jn, u // 2 + 1)
                unit(u, jn)

            for u in range(4):
                split_and_unit(u, 0)
            dve.wait_ge(gate_turned, 2)
            for kind, row in ((BETA, ROW_BETA), (G_SUM, ROW_G)):
                nc.vector.tensor_copy(gates_all[:, kind, :, :], turned_gates(row)).then_inc(gates_ready, 1)
            for u in range(4, 10):
                split_and_unit(u, 0)
            first_stage_over(dve)

            def head(j, with_gemm):
                base = j * ND + 1
                nc.vector.tensor_copy(g_head[:, :, :], gates_all[:, :, bass.ds(j, 1), :].rearrange("p k h t -> p k (h t)")).then_inc(head_gates, 1)
                if with_gemm:
                    dve.wait_ge(conv_step, j * 6 * TAPS + 6 * TAPS)
                    head_taps_copy(j + 1)
                dve.wait_ge(head_gates, j + 1)
                for step in PREP:
                    what, g, lev = step
                    if what in ("out", "split"):
                        ahead, u = PREP_UNITS[g] if g < len(PREP_UNITS) else (1, SCAN_UNITS[0])
                        if what == "out" and (with_gemm or not ahead):
                            unit(u, j + ahead)
                        elif what == "split" and (with_gemm or not ahead):
                            split_lo(j + ahead, u // 2)
                        elif what == "out":
                            w_out_lo(u)
                        continue
                    if what not in DVE_READS:
                        continue
                    src = bank4(FILL[step] - 1)
                    four = slice(4 * g, 4 * g + 4)
                    if what in ("k", "q"):
                        side = 0 if what == "k" else 1
                        dst = kn if what == "k" else qn
                        dve.wait_ge(act_prep, j * NA + ACT_PREP[("square", what, g)])
                        nc.vector.tensor_reduce(sums[:, side, :], dst[:, :, :], AX_X, ALU.add).then_inc(norm_sum, 1)
                        dve.wait_ge(norm_sum, j * 4 + 2 * g + side + 1)
                        nc.vector.tensor_scalar(means[:, side, :], sums[:, side, :], EPS, None, ALU.add).then_inc(dve_prep, 1)
                        dve.wait_ge(pool_prep, j * NP_ + POOL_PREP[("power", what, g)])
                        nc.vector.scalar_tensor_tensor(out=dst[:, :, :], in0=src, scalar=1.0 if what == "k" else GDN_DIM ** -0.5,
                                                       in1=wide(powers[:, side, :], P), op0=ALU.mult, op1=ALU.mult).then_inc(dve_prep, 1)
                        continue
                    dve.wait_ge(filled, j * NFILL + FILL[step])
                    if what == "v":
                        nc.vector.tensor_tensor(vb[:, g, :, :], src, wide(g_head[:, BETA, four], P), ALU.mult).then_inc(dve_prep, 1)
                    elif what in ("N", "A"):
                        dve.wait_ge(act_prep, j * NA + ACT_PREP[("decay", 0, 0)])
                        dst = n_low[:, g, :, :] if what == "N" else a_t[:, four, :]
                        nc.vector.tensor_tensor(dst, src, decay[:, four, :], ALU.mult).then_inc(dve_prep, 1)
                    elif what == "M0":
                        nc.vector.tensor_tensor(t_inv[:, g, :, :], stacked(ident, 4), src, ALU.subtract).then_inc(dve_prep, 1)
                    elif what == "TX":
                        nc.vector.tensor_tensor(t_inv[:, g, :, :], t_inv[:, g, :, :], src, ALU.subtract).then_inc(dve_prep, 1)
                    elif what == "XR":
                        nc.vector.tensor_tensor(r_inv[:, g, :, :], r_inv[:, g, :, :], src, ALU.subtract).then_inc(dve_prep, 1)
                    elif what == "U":
                        nc.vector.tensor_copy(xb[:, g, :, :], src).then_inc(dve_prep, 1)

                def p_chunk(i, c):
                    n = FOX_CHUNK[(i, c)]
                    if n % 2 == 0:
                        return
                    nb = min(4, FOX_TILES[i][1] + 1 - 4 * c)
                    dve.wait_ge(fox_turned, j * NFC + n + 1)
                    if n >= 2:
                        dve.wait_ge(fox_pv, j * NFC + n - 1)
                    nc.vector.tensor_copy(probs_t[1][:, 0:nb, :], fox_t[:, 0:nb * P].rearrange("p (t d) -> p t d", t=nb)).then_inc(pt_dve, 1)

                nc.vector.memset(state[:, :], 0.0).then_inc(state_ready, 1)
                for i in range(NCHUNK + 1):
                    if i < NCHUNK:
                        rows, (g, tt) = slice(64 * (i % 2), 64 * (i % 2) + 64), divmod(i // 2, 4)
                        dve.wait_ge(scan_v, j * NCHUNK + i + 1)
                        nc.vector.tensor_tensor(v_new[rows, :], xb[rows, g, tt, :], scan_a[rows, 0:P], ALU.subtract).then_inc(v_new_ready, 1)
                        nk = (FOX_TILES[i][1] + 1) * P
                        dve.wait_ge(fox_scored, j * NFT + i + 1)
                        if i == 0 or i == NT:
                            dve.wait_ge(cum_row_loaded, j * 32 + 16 * (i // NT + 1))
                        if i >= 2:
                            dve.wait_ge(fox_pv, j * NFC + FOX_CHUNK[(i - 2, FOX_TILES[i - 2][1] // 4)] + 1)
                        nc.vector.memset(wait_holder[:, :], 0.0)
                        nc.vector.tensor_tensor_reduce(out=probs[i % 2][:, 0:nk], in0=fox_s[:, 0:nk], in1=cum_row[:, 0:nk], scale=1.0,
                                                       scalar=LOWEST, op0=ALU.add, op1=ALU.max,
                                                       accum_out=row_max[:, i % 2:i % 2 + 1]).then_inc(fox_max, 1)
                        dve.wait_ge(fox_max, j * NFT + i + 2)
                        nc.vector.tensor_scalar(neg_max[:, i % 2:i % 2 + 1], row_max[:, i % 2:i % 2 + 1], -1.0, None, ALU.mult).then_inc(fox_neg_max, 1)
                        dve.wait_ge(scan_s, j * NCHUNK + i + 1)
                        nc.vector.scalar_tensor_tensor(out=state[:, :], in0=state[:, :], scalar=g_last[:, i:i + 1], in1=scan_a[:, P:2 * P],
                                                       op0=ALU.mult, op1=ALU.add).then_inc(state_ready, 1)
                    if i >= 1:
                        hh, qb = FOX_TILES[i - 1]
                        p_chunk(i - 1, 0)
                        if qb >= 4:
                            p_chunk(i - 1, 1)
                        dve.wait_ge(fox_exp, j * NFT + i)
                        nc.vector.reciprocal(row_inv[:, i - 1:i], row_sum[:, i - 1:i]).then_inc(fox_inv, 1)
                        if i == 1:
                            dve.wait_ge(stored, j * 32 + 32)
                        dve.wait_ge(fox_inv, j * NFT + i)
                        dve.wait_ge(fox_pv, j * NFC + FOX_CHUNK[(i - 1, qb // 4)] + 1)
                        nc.vector.tensor_scalar(fox_out[:, qb, hh, :], fox_o[:, 0:FOX_DIM], row_inv[:, i - 1:i], None, ALU.mult).then_inc(fox_read, 1)
                    if with_gemm and i in SCAN_OUTS:
                        unit(SCAN_OUTS[i], j + 1, 0, 1)
                    if with_gemm and i - 1 in SCAN_OUTS:
                        unit(SCAN_OUTS[i - 1], j + 1, 2, 3)
                t0 = j * 7
                dve.wait_ge(tail_square, j * 2 + 1)
                nc.vector.tensor_reduce(tail_ss[:, 0:16], probs[0][:, :].rearrange("p (a d) -> p a d", d=FOX_DIM), AX_X, ALU.add).then_inc(tail_dve, 1)
                dve.wait_ge(tail_square, j * 2 + 2)
                nc.vector.tensor_reduce(tail_ss[:, 16:16 + NT], probs[1][:, :].rearrange("p (a d) -> p a d", d=GDN_DIM), AX_X, ALU.add).then_inc(tail_dve, 1)
                dve.wait_ge(tail_dve, t0 + 2)
                nc.vector.tensor_scalar(tail_ms[:, 0:16], tail_ss[:, 0:16], 1.0 / FOX_DIM, EPS, ALU.mult, ALU.add).then_inc(tail_dve, 1)
                nc.vector.tensor_scalar(tail_ms[:, 16:16 + NT], tail_ss[:, 16:16 + NT], 1.0 / GDN_DIM, EPS, ALU.mult, ALU.add).then_inc(tail_dve, 1)
                dve.wait_ge(tail_power, j * 2 + 2)
                fo = fox_out[:, :, :, :].rearrange("p t h d -> p (t h) d")
                nc.vector.tensor_tensor(fo, fo, wide(tail_rs[:, 0:16], FOX_DIM), ALU.mult).then_inc(tail_dve, 1)
                nc.vector.tensor_tensor(u_all, u_all, wide(tail_rs[:, 16:16 + NT], GDN_DIM), ALU.mult).then_inc(tail_dve, 1)
                dve.wait_ge(tail_dve, t0 + 5)
                nc.vector.tensor_tensor(fo, fo, stacked(fox_norm_row[:, :], 16), ALU.mult).then_inc(mixed_ready, 1)
                dve.wait_ge(tail_dve, t0 + 6)
                nc.vector.tensor_tensor(u_all, u_all, stacked(gdn_norm_row[:, :], NT), ALU.mult).then_inc(tail_dve, 1)
                dve.wait_ge(tail_dve, t0 + 7)
                nc.vector.tensor_tensor(u_all, u_all, z_tok[:, :, :], ALU.mult).then_inc(mixed_ready, 1)

            def w_out_lo(c):
                g = gemm_block(GDN_HEADS, c)
                dve.wait_ge(w_hi_ready, g + 1)
                dve.wait_ge(w_lo_ready, g)
                cols = slice(c * P, (c + 1) * P)
                nc.vector.tensor_tensor(big_lo[:, :, cols], w_raw[slot_of(c)][:, :, :], big_hi[:, :, cols].bitcast(F32), ALU.subtract).then_inc(w_lo_ready, 1)

            with dve.Fori(0, GDN_HEADS - 1) as j:
                head(j, True)
            head(GDN_HEADS - 1, False)
            head_loop_over(dve)

            def m_lo_part(t):
                dve.wait_ge(m_hi_ready, t + 1)
                nc.vector.tensor_tensor(m_lo[t % 2][:, :, :], fox_s.rearrange("p (k m) -> p k m", k=KT), m_hi[t % 2][:, :, :].bitcast(F32),
                                        ALU.subtract).then_inc(m_lo_ready, 1)

            def h2_lo_part(t):
                dve.wait_ge(h2_hi_ready, t + 1)
                cols = slice(t * P, (t + 1) * P)
                nc.vector.tensor_tensor(h2_lo[:, :, cols], banks(6, 2).rearrange("p (k m) -> p k m", k=KT), h2_hi[:, :, cols].bitcast(F32),
                                        ALU.subtract).then_inc(h2_lo_ready, 1)

            m_lo_part(0)
            for t in range(NT):
                if t + 1 < NT:
                    m_lo_part(t + 1)
                y = y_buf[t % 2][:, :]
                dve.wait_ge(o_square, 2 * t + 1)
                nc.vector.tensor_scalar(o_ms[:, t:t + 1], o_ss[:, t:t + 1], 1.0 / D, EPS, ALU.mult, ALU.add).then_inc(o_mean, 1)
                if t >= 1:
                    h2_lo_part(t - 1)
                if t == 0:
                    dve.wait_ge(late_loaded, 48)
                dve.wait_ge(o_power, 2 * t + 1)
                nc.vector.scalar_tensor_tensor(out=y, in0=out_banks(t), scalar=o_rs[:, t:t + 1], in1=post_mix_row[:, :],
                                               op0=ALU.mult, op1=ALU.mult).then_inc(y_done, 1)
                dve.wait_ge(y_done, t + 1)
                nc.vector.tensor_tensor(x_new[:, t, :], x_new[:, t, :], y, ALU.add).then_inc(x_new_ready, 1)
                dve.wait_ge(o_square, 2 * t + 2)
                nc.vector.tensor_scalar(o_ms[:, NT + t:NT + t + 1], o_ss[:, NT + t:NT + t + 1], 1.0 / D, EPS, ALU.mult, ALU.add).then_inc(o_mean, 1)
                dve.wait_ge(o_power, 2 * t + 2)
                nc.vector.scalar_tensor_tensor(out=y, in0=x_new[:, t, :], scalar=o_rs[:, NT + t:NT + t + 1], in1=pre_mlp_row[:, :],
                                               op0=ALU.mult, op1=ALU.mult).then_inc(h2_normed, 1)
            h2_lo_part(NT - 1)

            def up_lo(h, f, s):
                dve.wait_ge(mlp_hi, f + (h * STEPS + 1))
                nc.vector.tensor_tensor(u_lo[s][:, :, :], w_raw[s][:, :, :], u_hi[s][:, :, :].bitcast(F32), ALU.subtract).then_inc(mlp_lo, 1)

            def square(h, f, s):
                a = act_ff[:, bass.ds(f, 1), :].rearrange("p a t -> p (a t)")
                dve.wait_ge(relu_done, f + (h * FT + 1))
                nc.vector.tensor_tensor(a, a, a, ALU.mult).then_inc(square_done, 1)

            def down_lo(h, f, s):
                up_lo(h, f + FT, s)
                dve.wait_ge(act_hi, f + (h * FT + 1))
                nc.vector.tensor_tensor(a_lo[s][:, :], act_ff[:, bass.ds(f, 1), :].rearrange("p a t -> p (a t)"), a_hi[s][:, :].bitcast(F32),
                                        ALU.subtract).then_inc(act_lo, 1)

            def out_of_down(h):
                dve.wait_ge(mlp_done, (h + 1) * STEPS)
                for m in range(1, KT, 2):
                    nc.vector.tensor_copy(down_T[:, m, :], banks(m)).then_inc(down_dve, 1)

            def finish(h, tts):
                dve.wait_ge(late_loaded, 64)
                for tt in tts:
                    t = h * HT + tt
                    dve.wait_ge(o_square, 2 * NT + t + 1)
                    nc.vector.tensor_scalar(o_ms[:, 2 * NT + t:2 * NT + t + 1], o_ss[:, 2 * NT + t:2 * NT + t + 1], 1.0 / D, EPS, ALU.mult, ALU.add).then_inc(o_mean, 1)
                    dve.wait_ge(o_power, 2 * NT + t + 1)
                    if t >= 2:
                        dve.wait_ge(out_stored[t % 2], 16 * (t // 2))
                    nc.vector.scalar_tensor_tensor(out=final[tt % 2], in0=final_banks(tt), scalar=o_rs[:, 2 * NT + t:2 * NT + t + 1],
                                                   in1=post_mlp_row[:, :], op0=ALU.mult, op1=ALU.mult).then_inc(final_step, 1)
                    dve.wait_ge(final_step, t + 1)
                    nc.vector.tensor_tensor(final[tt % 2], final[tt % 2], x_new[:, t, :], ALU.add).then_inc(final_ready, 1)

            for h in range(2):
                up_lo(h, 0, 0)
                up_lo(h, 1, 1)
                square(h, 0, 0)
                if h == 1:
                    finish(0, range(0, 2))
                    finish(0, range(2, HT))
                with dve.Fori(1, FT // 2) as i:
                    up_lo(h, i * 2, 0)
                    square(h, i * 2 - 1, 1)
                    up_lo(h, i * 2 + 1, 1)
                    square(h, i * 2, 0)
                square(h, FT - 1, 1)
                with dve.Fori(0, FT // 2) as i:
                    down_lo(h, i * 2, 0)
                    down_lo(h, i * 2 + 1, 1)
                out_of_down(h)
            finish(1, range(HT))

        @block.gpsimd
        def _(pool):
            nc.gpsimd.memset(w_raw[0][:, :, :], 0.0).then_inc(gate_w_cleared, 1)
            nc.gpsimd.memset(row_bias[:, :], 0.0).then_inc(params_cleared, 1)
            nc.gpsimd.memset(row_a[:, :], 0.0).then_inc(params_cleared, 1)
            nc.gpsimd.memset(zeros[:, :], 0.0).then_inc(half_ready, 1)
            nc.gpsimd.memset(minus_half[:, :], -0.5).then_inc(half_ready, 1)
            nc.gpsimd.memset(gate_in[:, :], 0.0).then_inc(gate_pool, 1)
            pool.wait_ge(half_ready, 2)
            for t in range(NT):
                pool.wait_ge(x_mean, t + 1)
                nc.gpsimd.tensor_tensor(x_rs[:, t:t + 1], x_ms[:, t:t + 1], minus_half[:, 0:1], ALU.pow).then_inc(x_power, 1)
            first_stage_over(pool)

            def head(j, with_gemm):
                base = j * NP_
                pool.wait_ge(head_gates, j + 1)
                for step in PREP:
                    what, g, lev = step
                    four = slice(4 * g, 4 * g + 4)
                    if what in ("k", "q"):
                        side = 0 if what == "k" else 1
                        pool.wait_ge(dve_prep, j * ND + 1 + DVE_PREP[("mean", what, g)])
                        nc.gpsimd.tensor_tensor(powers[:, side, :], means[:, side, :], minus_half[:, 0:4], ALU.pow).then_inc(pool_prep, 1)
                    elif what == "decay":
                        pool.wait_ge(act_prep, j * NA + ACT_PREP[("gl", 0, 0)])
                        nc.gpsimd.tensor_tensor(decay[:, :, :], decay[:, :, :], wide(g_head[:, G_SUM, :], P), ALU.subtract).then_inc(pool_prep, 1)
                        pool.wait_ge(pool_prep, base + POOL_PREP[("decay", 1)])
                        nc.gpsimd.tensor_tensor(decay[:, :, :], decay[:, :, :], stacked(const[:, DECAY_MASK, :], NT), ALU.add).then_inc(pool_prep, 1)
                    elif what == "knT":
                        pool.wait_ge(dve_prep, j * ND + 1 + DVE_PREP[("k", g, 0)])
                        nc.gpsimd.tensor_tensor(kd[:, four, :], kn[:, :, :], wide(g_head[:, G_REST, four], P), ALU.mult).then_inc(pool_prep, 1)
                        pool.wait_ge(filled, j * NFILL + FILL[step])
                        pool.wait_ge(pool_prep, base + POOL_PREP[("kd", g)])
                        nc.gpsimd.tensor_tensor(kn[:, :, :], kn[:, :, :], wide(g_head[:, BETA, four], P), ALU.mult).then_inc(pool_prep, 1)
                        pool.wait_ge(pool_prep, base + POOL_PREP[("kb", g)])
                        nc.gpsimd.tensor_tensor(kbg[:, g, :, :], kn[:, :, :], wide(g_head[:, G_EXP, four], P), ALU.mult).then_inc(pool_prep, 1)
                    elif what == "qnT":
                        pool.wait_ge(filled, j * NFILL + FILL[step])
                        nc.gpsimd.tensor_tensor(qn[:, :, :], qn[:, :, :], wide(g_head[:, G_EXP, four], P), ALU.mult).then_inc(pool_prep, 1)
                    elif what == "N":
                        pool.wait_ge(dve_prep, j * ND + 1 + DVE_PREP[step])
                        level(j, g, 0)
                        pool.wait_ge(pool_prep, base + POOL_PREP[("level", g, 0)])
                        nc.gpsimd.tensor_tensor(r_inv[:, g, :, :], stacked(ident, 4), n_lev[:, g, :, :], ALU.subtract).then_inc(pool_prep, 1)
                    elif what == "M0":
                        pool.wait_ge(filled, j * NFILL + FILL[step])
                        pool.wait_ge(pool_prep, base + POOL_PREP[("R0", g)])
                        level(j, g, 1)
                    elif what == "X" and lev < LEVELS - 1:
                        pool.wait_ge(filled, j * NFILL + FILL[step])
                        level(j, g, lev + 1)
                for i, (hh, qb) in enumerate(FOX_TILES):
                    hr = head_rows(hh)
                    pool.wait_ge(q_hi_ready, (j * NFT + i) * 2 + 2)
                    if i >= 2:
                        pool.wait_ge(fox_scored, j * NFT + i - 1)
                    nc.gpsimd.tensor_tensor(q_lo[i % 2][hr, :], q_fox[hr, qb * P:(qb + 1) * P], q_hi[i % 2][hr, :].bitcast(F32),
                                            ALU.subtract).then_inc(q_ready, 1)
                    if i - 1 in (SCAN_SPLITS if with_gemm else W_OUT_STEPS):
                        pool.wait_ge(q_ready, j * NFT + i + 1)
                    if with_gemm and i - 1 in SCAN_SPLITS:
                        split_lo(j + 1, SCAN_SPLITS[i - 1])
                    if not with_gemm and i - 1 in W_OUT_STEPS:
                        w_out_lo(W_OUT_STEPS[i - 1])
                pool.wait_ge(tail_dve, j * 7 + 4)
                nc.gpsimd.tensor_tensor(tail_rs[:, 0:16], tail_ms[:, 0:16], minus_half[:, :], ALU.pow).then_inc(tail_power, 1)
                nc.gpsimd.tensor_tensor(tail_rs[:, 16:16 + NT], tail_ms[:, 16:16 + NT], minus_half[:, 0:NT], ALU.pow).then_inc(tail_power, 1)

            def level(j, g, lev):
                nc.gpsimd.tensor_tensor(n_lev[:, g, :, :], n_low[:, g, :, :], stacked(const[:, LEVEL_MASK + lev, :], 4), ALU.mult).then_inc(pool_prep, 1)

            def split_lo(jn, b):
                g = gemm_block(jn, b)
                pool.wait_ge(w_hi_ready, g + 1)
                pool.wait_ge(w_lo_ready, g)
                nc.gpsimd.tensor_tensor(w_lo[slot_of(b)][:, :, :], w_raw[slot_of(b)][:, :, :], w_hi[slot_of(b)][:, :, :].bitcast(F32),
                                        ALU.subtract).then_inc(w_lo_ready, 1)
                pool.wait_ge(w_lo_ready, g + 1)

            def w_out_lo(c):
                g = gemm_block(GDN_HEADS, c)
                cols = slice(c * P, (c + 1) * P)
                pool.wait_ge(w_hi_ready, g + 1)
                pool.wait_ge(w_lo_ready, g)
                nc.gpsimd.tensor_tensor(big_lo[:, :, cols], w_raw[slot_of(c)][:, :, :], big_hi[:, :, cols].bitcast(F32),
                                        ALU.subtract).then_inc(w_lo_ready, 1)
                pool.wait_ge(w_lo_ready, g + 1)

            with pool.Fori(0, GDN_HEADS - 1) as j:
                head(j, True)
            head(GDN_HEADS - 1, False)
            head_loop_over(pool)
            nc.gpsimd.memset(halves[:, :], -0.5).then_inc(half_ready, 1)
            pool.wait_ge(half_ready, 3)
            for n in range(3 * NT):
                col = (n // 2 + NT * (n % 2)) if n < 2 * NT else n
                pool.wait_ge(o_mean, n + 1)
                nc.gpsimd.tensor_tensor(o_rs[:, col:col + 1], o_ms[:, col:col + 1], halves[:, 0:1], ALU.pow).then_inc(o_power, 1)

        @block.tensor
        def _(pe):
            def unit_part(s, n, k):
                rhs_hi = big_hi[:, k, n * HALF:(n + 1) * HALF]
                rhs_lo = big_lo[:, k, n * HALF:(n + 1) * HALF]
                acc = banks(n)
                nc.tensor.matmul(acc, w_hi[s][:, k, :], rhs_hi, start=(k == 0), stop=False)
                nc.tensor.matmul(acc, w_hi[s][:, k, :], rhs_lo, start=False, stop=False)
                last = nc.tensor.matmul(acc, w_lo[s][:, k, :], rhs_hi, start=False, stop=(k == KT - 1))
                if k == KT - 1:
                    last.then_inc(gemm_done, 1)

            def half_block_out(jn, b, n):
                if b > 0:
                    pe.wait_ge(gemm_read, reads_done(jn, b - 1, n))
                elif isinstance(jn, int) and jn == 0:
                    pe.wait_ge(gemm_read, n + 1)
                else:
                    pe.wait_ge(k_lo_ready, jn * 4 - 2 + 2 * n)

            def unit(u, jn):
                for k in range(KT):
                    part(u, jn, k)

            def part(u, jn, k):
                b, n = u // 2, u % 2
                if k == 0:
                    if n == 0:
                        pe.wait_ge(w_lo_ready, gemm_block(jn, b) + 1)
                    half_block_out(jn, b, n)
                unit_part(slot_of(b), n, k)

            pe.wait_ge(params_loaded, PARAM_LOADS * 16)
            for t in range(NT):
                pe.wait_ge(x_normed, t + 1)
                if t >= 2:
                    pe.wait_ge(x_lo, t - 1)
                for k in range(KT):
                    last = nc.tensor.transpose(banks(2 + 2 * (t % 2), 2)[:, k * P:(k + 1) * P], x_n[t % 2][:, k * P:(k + 1) * P], ident)
                last.then_inc(x_turned, 1)
            pe.wait_ge(x_lo, NT)
            pe.wait_ge(w_lo_ready, 1)
            nc.tensor.transpose(fox_t[:, 0:TAPS * 3 * GDN_HEADS], conv_rows[:, :], ident[0:TAPS * 3 * GDN_HEADS, 0:TAPS * 3 * GDN_HEADS]).then_inc(gate_turned, 1)
            for n in range(2):
                for k in range(KT):
                    unit_part(0, n, k)
            for u in range(4):
                unit(u, 0)
            pe.wait_ge(gate_dve, GATE_ROWS_DONE)
            for t in range(NT):
                last = nc.tensor.transpose(banks(2, 2)[:, t * P:(t + 1) * P], gate_rows[:, t * P:(t + 1) * P], ident)
            last.then_inc(gate_turned, 1)
            for u in range(4, 10):
                unit(u, 0)
            first_stage_over(pe)

            def four_products(f, lhs, rhs):
                for i in range(4):
                    last = nc.tensor.matmul(bank(f)[:, i * P:(i + 1) * P], lhs(i), rhs(i), start=True, stop=True)
                last.then_inc(filled, 1)

            def four_turned(f, src):
                for i in range(4):
                    last = nc.tensor.transpose(bank(f)[:, i * P:(i + 1) * P], src(i), ident)
                last.then_inc(filled, 1)

            def head(j, with_gemm):
                pe.wait_ge(fox_read, j * NFT + 1)

                def after_act(name):
                    pe.wait_ge(act_prep, j * NA + ACT_PREP[name])

                def after_dve(name):
                    pe.wait_ge(dve_prep, j * ND + 1 + DVE_PREP[name])

                def after_pool(name):
                    pe.wait_ge(pool_prep, j * NP_ + POOL_PREP[name])

                for step in PREP:
                    what, g, lev = step
                    if what == "part":
                        unit_index, k = divmod(g, KT)
                        ahead, u = PREP_UNITS[unit_index]
                        if with_gemm or not ahead:
                            part(u, j + ahead, k)
                        continue
                    if what in ("gl", "decay", "out", "split"):
                        continue
                    if step == ("z", 0, 0):
                        pe.wait_ge(silu_done, j + 1)
                    f = FILL[step] - 1
                    if f >= NFILL_BANKS:
                        old = FILLS[f - NFILL_BANKS]
                        (after_act if old[0] in ACT_READS else after_dve)(old)
                    tok = [slice((4 * g + i) * P, (4 * g + i + 1) * P) for i in range(4)]
                    if what == "fv":
                        four_turned(f, lambda i: v_fox[:, tok[i]])
                    elif what in ("z", "k", "q", "v"):
                        kind = {"z": CZ, "k": CK, "q": CQ, "v": CV}[what]
                        four_turned(f, lambda i: c_raw[:, kind, tok[i]])
                    elif what == "knT":
                        after_dve(("k", g, 0))
                        four_turned(f, lambda i: kn[:, i, :])
                    elif what == "qnT":
                        after_dve(("q", g, 0))
                        four_turned(f, lambda i: qn[:, i, :])
                    elif what == "qdT":
                        after_pool(("qd", g))
                        four_turned(f, lambda i: qn[:, i, :])
                    elif what == "kbT":
                        after_pool(("kb", g))
                        four_turned(f, lambda i: kn[:, i, :])
                    elif what == "N":
                        after_act(("kbT", g, 0))
                        four_products(f, lambda i: knT[:, i, :], lambda i: kbT[:, i, :])
                    elif what == "A":
                        four_products(f, lambda i: knT[:, i, :], lambda i: qnT[:, i, :])
                    elif what == "M0":
                        after_pool(("level", g, 0))
                        four_turned(f, lambda i: n_lev[:, g, i, :])
                    elif what == "X":
                        after_pool(("level", g, lev))
                        after_dve(("TX", g, lev - 1) if lev > 1 else ("M0", g, 0))
                        four_products(f, lambda i: n_lev[:, g, i, :], lambda i: t_inv[:, g, i, :])
                    elif what == "TX":
                        after_act(("X", g, lev))
                        if lev > 1:
                            after_dve(("XR", g, lev - 1))
                        four_products(f, lambda i: r_inv[:, g, i, :], lambda i: xb[:, g, i, :])
                    elif what == "XR":
                        after_act(("X", g, lev))
                        if lev > 1:
                            after_dve(("XR", g, lev - 1))
                        four_products(f, lambda i: xb[:, g, i, :], lambda i: r_inv[:, g, i, :])
                    elif what == "W":
                        after_dve(("XR", g, LEVELS - 1))
                        four_products(f, lambda i: kbg[:, g, i, :], lambda i: r_inv[:, g, i, :])
                    elif what == "U":
                        four_products(f, lambda i: r_inv[:, g, i, :], lambda i: vb[:, g, i, :])

                after_act(("W", 1, 0))
                after_dve(("U", 1, 0))

                def turn(i, c):
                    n = FOX_CHUNK[(i, c)]
                    if n >= 1:
                        pe.wait_ge(*((pt_act, j * (NFC // 2) + (n - 1) // 2 + 1) if n % 2 == 1 else (pt_dve, j * (NFC // 2) + n // 2)))
                    for kb in range(4 * c, min(4 * c + 4, FOX_TILES[i][1] + 1)):
                        last = nc.tensor.transpose(fox_t[:, (kb - 4 * c) * P:(kb - 4 * c + 1) * P], probs[i % 2][:, kb * P:(kb + 1) * P], ident)
                    last.then_inc(fox_turned, 1)

                def times_v(i, c):
                    n, (hh, qb) = FOX_CHUNK[(i, c)], FOX_TILES[i]
                    pe.wait_ge(*((pt_act, j * (NFC // 2) + n // 2 + 1) if n % 2 == 0 else (pt_dve, j * (NFC // 2) + n // 2 + 1)))
                    if c == 0:
                        pe.wait_ge(fox_read, j * NFT + i + 1)
                    for kb in range(4 * c, min(4 * c + 4, qb + 1)):
                        last = nc.tensor.matmul(fox_o[:, 0:FOX_DIM], probs_t[n % 2][:, kb - 4 * c, :], v_tok[:, kb, hh * FOX_DIM:(hh + 1) * FOX_DIM],
                                                start=(kb == 0), stop=(kb == qb))
                    last.then_inc(fox_pv, 1)

                def beside_scan(i, n):
                    if with_gemm and i < NCHUNK:
                        unit_index, k = divmod(SCAN_STEP_PARTS * i + n, KT)
                        part(SCAN_UNITS[unit_index], j + 1, k)

                for i in range(NCHUNK + 1):
                    if i < NCHUNK:
                        half = 64 * (i % 2)
                        rows, (g, tt) = slice(half, half + 64), divmod(i // 2, 4)
                        toks = slice(half, half + 64)
                        pe.wait_ge(state_ready, j * (NCHUNK + 1) + i + 1)
                        nc.tensor.matmul(scan_a[rows, 0:P], t_inv[:, g, tt, toks], state[:, :], start=True, stop=True).then_inc(scan_v, 1)
                        if i >= 2:
                            pe.wait_ge(o_read, j * NCHUNK + i - 1)
                        nc.tensor.matmul(scan_b[rows, 0:P], qdT[:, i // 2, toks], state[:, :], start=True, stop=False)
                        hh, qb = FOX_TILES[i]
                        hr = head_rows(hh)
                        pe.wait_ge(q_ready, j * NFT + i + 1)
                        if i == 0:
                            pe.wait_ge(k_lo_ready, j * 4 + 4)
                        else:
                            pe.wait_ge(fox_max, j * NFT + i + 1)
                        nk = (qb + 1) * P
                        for c in range(0, nk, 512):
                            ce = min(c + 512, nk)
                            nc.tensor.matmul(fox_s[:, c:ce], q_hi[i % 2][:, :], k_split[hh][:, c:ce], start=True, stop=False)
                            nc.tensor.matmul(fox_s[:, c:ce], q_lo[i % 2][hr, :], k_split[hh][hr, c:ce], start=False, stop=True)
                        nc.tensor.matmul(fox_s[:, qb * P:nk], ident_bf[:, :], causal_bf[:, :], start=False, stop=True,
                                         skip_group_check=True).then_inc(fox_scored, 1)
                    beside_scan(i, 0)
                    if i >= 1:
                        pe.wait_ge(fox_exp, j * NFT + i)
                        turn(i - 1, 0)
                    if i < NCHUNK:
                        pe.wait_ge(v_new_ready, j * NCHUNK + i + 1)
                        nc.tensor.matmul(scan_a[:, P:2 * P], kd[rows, i // 2, :], v_new[rows, :], start=True, stop=True).then_inc(scan_s, 1)
                        nc.tensor.matmul(scan_b[rows, 0:P], a_t[rows, i // 2, toks], v_new[rows, :], start=False, stop=True).then_inc(scan_o, 1)
                    beside_scan(i, 1)
                    if i >= 1:
                        if FOX_TILES[i - 1][1] >= 4:
                            turn(i - 1, 1)
                        times_v(i - 1, 0)
                        if FOX_TILES[i - 1][1] >= 4:
                            times_v(i - 1, 1)
                    beside_scan(i, 2)

            with pe.Fori(0, GDN_HEADS - 1) as j:
                head(j, True)
            head(GDN_HEADS - 1, False)
            head_loop_over(pe)
            pe.wait_ge(w_lo_ready, W_OUT_SPLIT)

            def turn_mixed(t):
                pe.wait_ge(w_loaded[t % 2], 16 * (SLOT_LOADS[t % 2] - NT // 2 + t // 2 + 1))
                if t >= 1:
                    pe.wait_ge(m_lo_ready, t)
                for k in range(KT):
                    last = nc.tensor.transpose(fox_s[:, k * P:(k + 1) * P], w_raw[t % 2][:, k, :], ident)
                last.then_inc(m_turned, 1)

            def turn_h2(t):
                pe.wait_ge(h2_normed, t + 1)
                if t >= 1:
                    pe.wait_ge(h2_lo_ready, t)
                for k in range(KT):
                    last = nc.tensor.transpose(banks(6, 2)[:, k * P:(k + 1) * P], y_buf[t % 2][:, k * P:(k + 1) * P], ident)
                last.then_inc(h2_turned, 1)

            turn_mixed(0)
            for t in range(NT):
                if t + 1 < NT:
                    turn_mixed(t + 1)
                pe.wait_ge(m_lo_ready, t + 1)
                if t >= 2:
                    pe.wait_ge(y_done, t - 1)
                for n in range(2):
                    acc = banks(2 * (t % 2) + n)
                    cols = slice(n * HALF, (n + 1) * HALF)
                    for k in range(KT):
                        nc.tensor.matmul(acc, m_hi[t % 2][:, k, :], big_hi[:, k, cols], start=(k == 0), stop=False)
                        nc.tensor.matmul(acc, m_hi[t % 2][:, k, :], big_lo[:, k, cols], start=False, stop=False)
                        last = nc.tensor.matmul(acc, m_lo[t % 2][:, k, :], big_hi[:, k, cols], start=False, stop=(k == KT - 1))
                last.then_inc(out_done, 1)
                if t >= 1:
                    turn_h2(t - 1)
            turn_h2(NT - 1)

            def up(h, f, s, wait):
                pe.wait_ge(mlp_lo, f + (h * STEPS + 1))
                if wait:
                    pe.wait_ge(relu_done, f + (h * FT - 1))
                toks = slice(h * HALF, (h + 1) * HALF)
                for k in range(KT):
                    nc.tensor.matmul(banks(s), u_hi[s][:, k, :], h2_hi[:, k, toks], start=(k == 0), stop=False)
                    nc.tensor.matmul(banks(s), u_hi[s][:, k, :], h2_lo[:, k, toks], start=False, stop=False)
                    last = nc.tensor.matmul(banks(s), u_lo[s][:, k, :], h2_hi[:, k, toks], start=False, stop=(k == KT - 1))
                last.then_inc(mlp_done, 1)

            def down(h, f, s, first, final_step):
                pe.wait_ge(act_lo, f + (h * FT + 1))
                for m in range(KT):
                    nc.tensor.matmul(banks(m), u_hi[s][:, m, :], a_hi[s][:, :], start=first, stop=False)
                    nc.tensor.matmul(banks(m), u_hi[s][:, m, :], a_lo[s][:, :], start=False, stop=False)
                    last = nc.tensor.matmul(banks(m), u_lo[s][:, m, :], a_hi[s][:, :], start=False, stop=final_step)
                last.then_inc(mlp_done, 1)

            def turn_final(h, tts):
                pe.wait_ge(down_act, (h + 1) * KT // 2)
                pe.wait_ge(down_dve, (h + 1) * KT // 2)
                for tt in tts:
                    if tt >= 3:
                        pe.wait_ge(final_step, h * HT + tt - 2)
                    for m in range(KT):
                        last = nc.tensor.transpose(final_banks(tt)[:, m * P:(m + 1) * P], down_T[:, m, tt * P:(tt + 1) * P], ident)
                    last.then_inc(final_turned, 1)

            for h in range(2):
                if h == 0:
                    pe.wait_ge(h2_lo_ready, NT)
                    pe.wait_ge(y_done, NT)
                else:
                    pe.wait_ge(down_act, KT // 2)
                    pe.wait_ge(down_dve, KT // 2)
                up(h, 0, 0, False)
                up(h, 1, 1, False)
                if h == 1:
                    turn_final(0, range(0, 2))
                    turn_final(0, range(2, HT))
                with pe.Fori(1, FT // 2) as i:
                    up(h, i * 2, 0, True)
                    up(h, i * 2 + 1, 1, True)
                pe.wait_ge(relu_done, (h + 1) * FT)
                if h == 1:
                    pe.wait_ge(final_step, HT)
                down(h, 0, 0, True, False)
                down(h, 1, 1, False, False)
                with pe.Fori(1, FT // 2 - 1) as i:
                    down(h, i * 2, 0, False, False)
                    down(h, i * 2 + 1, 1, False, False)
                down(h, FT - 2, 0, False, False)
                down(h, FT - 1, 1, False, True)
            turn_final(1, range(HT))


_INS = ['x', 'pre_mix_norm', 'w_in', 'fox_f_bias', 'fox_out_norm', 'gdn_conv_w', 'gdn_a_log', 'gdn_dt_bias', 'gdn_out_norm',
        'w_out', 'post_mix_norm', 'pre_mlp_norm', 'w_up', 'w_down', 'post_mlp_norm']
_OUTS = [((1, SEQ, D), 'float32')]


def shape_constants():
    import numpy as np
    row, col = np.arange(P)[:, None], np.arange(P)[None, :]
    tiles = np.zeros((N_CONST + 1, P, P), np.float32)
    tiles[IDENT] = row == col
    same_chunk = row // CHUNK == col // CHUNK
    tiles[DECAY_MASK] = np.where(same_chunk & (col >= row), 0.0, -1e30)
    tiles[N_CONST] = np.where(col <= row, 0.0, -1e30)
    for lev in range(LEVELS):
        size = 2 ** lev
        tiles[LEVEL_MASK + lev] = (row // (2 * size) == col // (2 * size)) & (col // size % 2 == 1) & (row // size % 2 == 0)
    keep = np.ones((P, SEQ), np.float32)
    keep[ROW_G:ROW_G + 32, ::CHUNK] = 0.0
    return np.ascontiguousarray(tiles.transpose(1, 0, 2).reshape(P, (N_CONST + 1) * P)), keep


def kernel(**inputs):
    import numpy as _np
    import concourse.bacc as _bacc
    from concourse import mybir as _mybir
    from concourse.bass_utils import run_bass_kernel_spmd as _run

    nc = _bacc.Bacc("TRN2", target_bir_lowering=False, num_devices=1)
    given = {name: _np.ascontiguousarray(inputs[name]) for name in _INS}
    given["const_tiles"], given["scan_keep"] = shape_constants()
    arrays, args = {}, []
    for name, a in given.items():
        arrays[f"in_{name}_dram"] = a
        args.append(nc.dram_tensor(f"in_{name}_dram", a.shape, _mybir.dt.from_np(a.dtype), kind="ExternalInput").ap())
    for i, (shape, dtype) in enumerate(_OUTS):
        dt = _mybir.dt.from_np(_np.dtype(dtype))
        args.append(nc.dram_tensor(f"out_{i}_dram", shape, dt, kind="ExternalOutput").ap())
    args.append(nc.dram_tensor("mixed", (SEQ, P + D), F32, kind="Internal").ap())
    args.append(nc.dram_tensor("gate_dram", (FOX_HEADS + GDN_HEADS, SEQ), F32, kind="Internal").ap())
    build(nc, *args)
    r = _run(nc, [arrays], core_ids=[0])
    got = tuple(r.results[0][f"out_{i}_dram"] for i in range(len(_OUTS)))
    return got[0]
```

```python
from contextlib import ExitStack

import concourse.bass as bass
from concourse import mybir

F32 = mybir.dt.float32
F32R = mybir.dt.float32r
BF16 = mybir.dt.bfloat16
ALU = mybir.AluOpType
ACT = mybir.ActivationFunctionType
AX_X = mybir.AxisListType.X

P = 128
SEQ = 1024
D = 1024
KT = D // P
NT = SEQ // P
HALF = SEQ // 2
D_FF = 4 * D
FT = D_FF // P
CHUNK = 64
NCHUNK = SEQ // CHUNK
FOX_HEADS, FOX_DIM = 8, 64
GDN_HEADS, GDN_DIM = 4, 128
D_GDN = GDN_HEADS * GDN_DIM
D_FOX = FOX_HEADS * FOX_DIM
TAPS = 4
EPS = 1e-6
LEVELS = 6
LOWEST = -3.0e38

FQ, FK, FV, FF = 0, D_FOX, 2 * D_FOX, 3 * D_FOX
GQ = FF + FOX_HEADS
GK, GV = GQ + D_GDN, GQ + 2 * D_GDN
GB = GQ + 3 * D_GDN
GA = GB + GDN_HEADS
GZ = GA + GDN_HEADS

BLOCKS = (FV, GZ, GQ, GK, GV, FQ, FK)
NB = len(BLOCKS)
CONV_BLOCKS = (2, 3, 4)
CQ, CK, CV, CZ = range(4)

ROW_CUM, ROW_BETA, ROW_G, ROW_REST = 0, 32, 64, 96
BETA, MINUS_G, G_EXP, G_REST = range(4)

IDENT, DECAY_MASK, LEVEL_MASK = 0, 1, 2
N_CONST = 2 + LEVELS

PREP_FILLS = [
    ("gl", 0, 0), ("fv", 0, 0), ("fv", 1, 0),
    ("k", 0, 0), ("q", 0, 0), ("z", 0, 0), ("z", 1, 0), ("v", 0, 0), ("v", 1, 0),
    ("knT", 0, 0), ("kbT", 0, 0), ("decay", 0, 0), ("qnT", 0, 0), ("N", 0, 0), ("A", 0, 0), ("k", 1, 0),
    ("M0", 0, 0), ("qdT", 0, 0), ("q", 1, 0), ("X", 0, 1), ("knT", 1, 0), ("kbT", 1, 0),
    ("TX", 0, 1), ("XR", 0, 1), ("qnT", 1, 0), ("N", 1, 0), ("A", 1, 0), ("qdT", 1, 0),
    ("X", 0, 2),
    ("M0", 1, 0), ("TX", 0, 2), ("XR", 0, 2), ("X", 1, 1), ("X", 0, 3),
    ("TX", 1, 1), ("XR", 1, 1), ("TX", 0, 3), ("XR", 0, 3), ("X", 1, 2), ("X", 0, 4),
    ("TX", 1, 2), ("XR", 1, 2), ("TX", 0, 4), ("XR", 0, 4), ("X", 1, 3), ("X", 0, 5),
    ("TX", 1, 3), ("XR", 1, 3), ("XR", 0, 5), ("X", 1, 4), ("W", 0, 0), ("U", 0, 0),
    ("TX", 1, 4), ("XR", 1, 4), ("X", 1, 5), ("XR", 1, 5), ("W", 1, 0), ("U", 1, 0),
]
NFILL_BANKS = 6

PREP_UNITS = [(0, 10), (0, 11), (0, 12), (0, 13), (1, 0), (1, 1), (1, 2), (1, 3)]
SCAN_UNITS = [4, 5, 6, 7, 8, 9]
SCAN_STEP_PARTS = 3
OWN_STEPS = 4 * KT


def with_projection(fills):
    steps = len(PREP_UNITS) * KT
    out, step, due = [], 0, []

    def parts(count):
        nonlocal step
        for _ in range(count):
            out.append(("part", step, 0))
            unit, k = divmod(step, KT)
            if k == 0 and unit % 2 == 0 and unit + 2 < len(PREP_UNITS) + 1 and PREP_UNITS[unit][1] != 12:
                out.append(("split", unit + 2, 0))
            if k == KT - 1:
                due.append(("out", unit, 0))
                if PREP_UNITS[unit][1] == 13:
                    out.append(("split", unit + 1, 0))
            step += 1

    n, pause = 0, 0
    for fill in fills:
        out.append(fill)
        if fill[0] in ("gl", "decay"):
            continue
        n += 1
        while due:
            out.append(due.pop(0))
        if n == 2:
            parts(KT)
        elif n > 2:
            if step == OWN_STEPS and pause < 5:
                pause += 1
                continue
            left = len([f for f in fills if f[0] not in ("gl", "decay")]) - n + 1
            parts(1 if step < OWN_STEPS else max(1, (steps - step) // left))
    parts(steps - step)
    return out + due


PREP = with_projection(PREP_FILLS)


def numbered(names):
    return {name: n + 1 for n, name in enumerate(names)}


FILLS = [s for s in PREP_FILLS if s[0] not in ("gl", "decay")]
FILL = numbered(FILLS)
ACT_READS = ("fv", "z", "knT", "qnT", "qdT", "kbT", "X", "W")
DVE_READS = ("k", "q", "v", "N", "A", "M0", "TX", "XR", "U")

_act, _dve, _pool = [], [], []
for _s in PREP_FILLS:
    _w, _g, _l = _s
    if _w in ("k", "q"):
        _act.append(("square", _w, _g))
        _dve += [("mean", _w, _g)] + ([("kb", _g)] if _w == "q" else []) + [_s]
        _pool.append(("power", _w, _g))
    elif _w == "gl":
        _act.append(_s)
        _pool.append(("decay", 0))
    elif _w == "decay":
        _act.append(_s)
    elif _w in ACT_READS:
        _act.append(_s)
    elif _w in DVE_READS:
        _dve.append(_s)
    if _w == "knT":
        _pool.append(("kd", _g))
    if _w == "kbT":
        _pool.append(("kbg", _g))
    if _w == "qnT":
        _pool.append(("qd", _g))
    if _w == "N":
        _pool += [("level", _g, 0), ("R0", _g)]
    if _w == "M0":
        _pool.append(("level", _g, 1))
    if _w == "X" and _l < LEVELS - 1:
        _pool.append(("level", _g, _l + 1))
ACT_PREP, DVE_PREP, POOL_PREP = numbered(_act), numbered(_dve), numbered(_pool)
NFILL, NA, ND, NP_ = len(FILLS), len(_act), len(_dve), len(_pool)

FOX_TILES = [(hh, qb) for hh in range(2) for qb in range(NT)]
FOX_CHUNKS = [(i, c) for i, (_, qb) in enumerate(FOX_TILES) for c in range(qb // 4 + 1)]
FOX_CHUNK = {c: n for n, c in enumerate(FOX_CHUNKS)}
NFT, NFC = len(FOX_TILES), len(FOX_CHUNKS)
SCAN_OUTS = {(KT * n + KT - 1) // SCAN_STEP_PARTS: u for n, u in enumerate(SCAN_UNITS)}
SCAN_SPLITS = {1: 3, 6: 4, 11: 5}
Z_STEP = 4
MEANS_STEP = 11
W_OUT_STEPS = {2: 4, 4: 5, 9: 6, 11: 7}


def gemm_block(jn, b):
    return 1 + NB * jn + b


def slot_of(b):
    return b % 2


def block_before_in_slot(g, b):
    if isinstance(g, int) and g <= 2:
        return -1 if g == 1 else 0
    return g - 1 if b == 0 else g - 3 if b == 1 else g - 2


READS = 2 * (NB - 1)


def reads_done(jn, b, n):
    return (jn * READS + 2 * b) + (n + 3)


def loads_before(jn, b):
    return (4 * jn + b // 2 + 1) if b % 2 == 0 else (3 * jn + b // 2 + 1)


def wide(ap, n):
    return ap.unsqueeze(2).to_broadcast([ap.shape[0], ap.shape[1], n])


def stacked(ap, n):
    return ap.unsqueeze(1).to_broadcast([ap.shape[0], n, ap.shape[1]])


def build(nc, x, pre_mix_norm, w_in, fox_f_bias, fox_out_norm, gdn_conv_w, gdn_a_log,
          gdn_dt_bias, gdn_out_norm, w_out, post_mix_norm, pre_mlp_norm, w_up, w_down,
          post_mlp_norm, const_tiles, scan_keep, out, mixed, gate_dram):
    x = x.rearrange("a s d -> (a s) d")
    out = out.rearrange("a s d -> (a s) d")
    w_in_k = w_in.rearrange("(k p) n -> p k n", p=P)
    w_out_k = w_out.rearrange("(k p) n -> p k n", p=P)
    w_up_k = w_up.rearrange("(k p) n -> p k n", p=P)
    with ExitStack() as ctx:
        def sem(name):
            return ctx.enter_context(nc.semaphore(name))

        def held(scope, name, shape, dt=F32):
            return scope.enter_context(nc.sbuf_tensor(name, shape, dt))

        ps = ctx.enter_context(nc.psum_tensor("ps", [P, 8 * 512], F32))

        def banks(first, count=1):
            return ps[:, first * 512:(first + count) * 512]

        gemm_ps = banks(0, 2)
        scan_a, scan_b, fox_s, fox_t, fox_o = banks(2), banks(3), banks(4, 2), banks(6), banks(7)
        fill_banks = [banks(2), banks(3), banks(4), banks(5), banks(6), banks(7)]

        whole = ctx.enter_context(ExitStack())
        const = held(whole, "const", [P, N_CONST, P])
        big = ctx.enter_context(ExitStack())
        big_hi = big.enter_context(nc.sbuf_tensor("big_hi", [P, KT, SEQ], F32R, side="right"))
        big_lo = big.enter_context(nc.sbuf_tensor("big_lo", [P, KT, SEQ], F32R, side="right"))
        w_raw = [held(whole, f"w_raw{s}", [P, KT, P]) for s in range(2)]
        w_hi = [held(whole, f"w_hi{s}", [P, KT, P], F32R) for s in range(2)]
        w_lo = [held(whole, f"w_lo{s}", [P, KT, P], F32R) for s in range(2)]
        ident = const[:, IDENT, :]

        mix = ExitStack()
        q_fox = held(mix, "q_fox", [P, SEQ])
        k_split = [held(mix, f"k_split{hh}", [P, SEQ], F32R) for hh in range(2)]
        v_fox = held(mix, "v_fox", [P, SEQ])
        c_raw = held(mix, "c_raw", [P, 4, SEQ])
        taps_in = held(mix, "taps_in", [P, TAPS - 1 + HALF])
        zeros = held(mix, "zeros", [P, TAPS - 1])
        wait_holder = held(mix, "wait_holder", [P, 1])
        minus_half = held(mix, "minus_half", [P, 16])
        gates_all = held(mix, "gates_all", [P, 4, GDN_HEADS, NT])
        conv_all = held(mix, "conv_all", [P, TAPS * 3 * GDN_HEADS])
        fox_norm_row = held(mix, "fox_norm_row", [P, FOX_DIM])
        gdn_norm_row = held(mix, "gdn_norm_row", [P, GDN_DIM])
        taps = held(mix, "taps", [P, TAPS, 3])
        ident_bf = held(mix, "ident_bf", [P, P], BF16)
        causal_bf = held(mix, "causal_bf", [P, P], BF16)

        params_cleared = sem("params_cleared")
        params_loaded = sem("params_loaded")
        pre_row_loaded = sem("pre_row_loaded")
        const_loaded = sem("const_loaded")
        x_loaded = [sem(f"x_loaded{s}") for s in range(4)]
        gate_w_cleared = sem("gate_w_cleared")
        gate_w_loaded = sem("gate_w_loaded")
        w_loaded = [sem(f"w_loaded{s}") for s in range(2)]
        x_square = sem("x_square")
        x_mean = sem("x_mean")
        x_power = sem("x_power")
        x_normed = sem("x_normed")
        x_turned = sem("x_turned")
        x_hi = sem("x_hi")
        x_lo = sem("x_lo")
        w_hi_ready = sem("w_hi_ready")
        w_lo_ready = sem("w_lo_ready")
        gemm_done = sem("gemm_done")
        gemm_read = sem("gemm_read")
        gate_act = sem("gate_act")
        gate_dve = sem("gate_dve")
        gate_pool = sem("gate_pool")
        gate_turned = sem("gate_turned")
        stored = sem("stored")
        gates_ready = sem("gates_ready")
        taps_ready = sem("taps_ready")
        conv_step = sem("conv_step")
        silu_done = sem("silu_done")
        head_gates = sem("head_gates")
        head_taps = sem("head_taps")
        g_row_loaded = sem("g_row_loaded")
        cum_row_loaded = sem("cum_row_loaded")
        filled = sem("filled")
        act_prep = sem("act_prep")
        dve_prep = sem("dve_prep")
        pool_prep = sem("pool_prep")
        norm_sum = sem("norm_sum")
        half_ready = sem("half_ready")
        scan_v = sem("scan_v")
        scan_o = sem("scan_o")
        scan_s = sem("scan_s")
        v_new_ready = sem("v_new_ready")
        state_ready = sem("state_ready")
        o_read = sem("o_read")
        k_hi_ready = sem("k_hi_ready")
        k_lo_ready = sem("k_lo_ready")
        q_copied = sem("q_copied")
        q_hi_ready = sem("q_hi_ready")
        q_ready = sem("q_ready")
        fox_scored = sem("fox_scored")
        fox_max = sem("fox_max")
        fox_neg_max = sem("fox_neg_max")
        fox_exp = sem("fox_exp")
        fox_turned = sem("fox_turned")
        pt_act = sem("pt_act")
        pt_dve = sem("pt_dve")
        fox_pv = sem("fox_pv")
        fox_inv = sem("fox_inv")
        fox_read = sem("fox_read")
        tail_square = sem("tail_square")
        tail_dve = sem("tail_dve")
        tail_power = sem("tail_power")
        z_normed = sem("z_normed")
        mixed_ready = sem("mixed_ready")

        first = ExitStack()
        x_in = [held(first, f"x_in{s}", [P, D]) for s in range(4)]
        x_n = [held(first, f"x_n{s}", [P, D]) for s in range(2)]
        x_sq = held(first, "x_sq", [P, D])
        x_ss = held(first, "x_ss", [P, NT])
        x_ms = held(first, "x_ms", [P, NT])
        x_rs = held(first, "x_rs", [P, NT])
        pre_row = held(first, "pre_row", [P, D])
        causal = held(first, "causal", [P, P])
        keep = held(first, "keep", [P, SEQ])
        conv_rows = held(first, "conv_rows", [TAPS * 3 * GDN_HEADS, P])
        row_bias = held(first, "row_bias", [P, 1])
        row_a = held(first, "row_a", [P, 2])
        gate_y = held(first, "gate_y", [P, SEQ])
        gate_u = held(first, "gate_u", [P, SEQ])
        gate_in = held(first, "gate_in", [P, SEQ])
        gate_rows = held(first, "gate_rows", [P, SEQ])
        first.close()

        cum_row = held(mix, "cum_row", [P, SEQ])
        decay = held(mix, "decay", [P, NT, P])
        v_tok = held(mix, "v_tok", [P, NT, P])
        z_tok = held(mix, "z_tok", [P, NT, P])
        kn = held(mix, "kn", [P, 4, P])
        qn = held(mix, "qn", [P, 4, P])
        kd = held(mix, "kd", [P, NT, P])
        kbg = held(mix, "kbg", [P, 2, 4, P])
        vb = held(mix, "vb", [P, 2, 4, P])
        knT = held(mix, "knT", [P, 4, P])
        qnT = held(mix, "qnT", [P, 4, P])
        kbT = held(mix, "kbT", [P, 4, P])
        qdT = held(mix, "qdT", [P, NT, P])
        n_low = held(mix, "n_low", [P, 2, 4, P])
        n_lev = held(mix, "n_lev", [P, 2, 4, P])
        t_inv = held(mix, "t_inv", [P, 2, 4, P])
        r_inv = held(mix, "r_inv", [P, 2, 4, P])
        xb = held(mix, "xb", [P, 2, 4, P])
        a_t = held(mix, "a_t", [P, NT, P])
        state = held(mix, "state", [P, P])
        v_new = held(mix, "v_new", [P, P])
        q_twice = [held(mix, f"q_twice{s}", [P, P]) for s in range(2)]
        q_hi = [held(mix, f"q_hi{s}", [P, P], F32R) for s in range(2)]
        q_lo = [held(mix, f"q_lo{s}", [P, P], F32R) for s in range(2)]
        probs = [m.rearrange("p g t d -> p (g t d)") for m in (n_low[:, :, :, :], n_lev[:, :, :, :])]
        probs_t = [held(mix, f"probs_t{s}", [P, 4, P]) for s in range(2)]
        fox_out = held(mix, "fox_out", [P, NT, 2, FOX_DIM])
        g_head = held(mix, "g_head", [P, 4, NT])
        g_last = held(mix, "g_last", [P, NCHUNK])
        sums = held(mix, "sums", [P, 2, 4])
        means = held(mix, "means", [P, 2, 4])
        powers = held(mix, "powers", [P, 2, 4])
        row_max = held(mix, "row_max", [P, 2])
        neg_max = held(mix, "neg_max", [P, 2])
        row_sum = held(mix, "row_sum", [P, NFT])
        row_inv = held(mix, "row_inv", [P, NFT])
        sq_scratch = held(mix, "sq_scratch", [P, FOX_DIM])
        sq_scratch2 = held(mix, "sq_scratch2", [P, GDN_DIM])
        tail_ss = held(mix, "tail_ss", [P, 16 + NT])
        tail_ms = held(mix, "tail_ms", [P, 16 + NT])
        tail_rs = tail_ms
        u_all = xb[:, :, :, :].rearrange("p g t d -> p (g t) d")
        w_all = t_inv[:, :, :, :].rearrange("p g t d -> p (g t) d")

        PARAM_LOADS = 8
        GATE_ROWS_DONE = 5

        def turned_gates(row):
            return banks(2, 2).rearrange("p (t r) -> p t r", r=P)[:, :, row:row + GDN_HEADS].rearrange("p t h -> p h t")

        def head_rows(hh):
            return slice(hh * FOX_DIM, (hh + 1) * FOX_DIM)

        TAIL_HALF = NT + NT // 2

        def tail_fox(hh):
            return hh * TAIL_HALF

        def tail_gdn(g):
            return g * TAIL_HALF + NT

        TAIL_SQUARES = (NT + NT // 2, NFT + NT)

        def bank(f):
            return fill_banks[f % NFILL_BANKS]

        def bank4(f):
            return bank(f).rearrange("p (t d) -> p t d", t=4)

        def first_stage_over(eng):
            eng.wait_ge(x_lo, NT)
            eng.wait_ge(gates_ready, 5)
            eng.wait_ge(stored, 32)

        mix.close()
        late = ctx.enter_context(ExitStack())
        h2_hi = held(late, "h2_hi", [P, KT, SEQ], F32R)
        h2_lo = held(late, "h2_lo", [P, KT, SEQ], F32R)
        x_new = held(late, "x_new", [P, NT, D])
        halves = held(late, "halves", [P, 2])
        o_ss = held(late, "o_ss", [P, 3 * NT])
        o_ms = held(late, "o_ms", [P, 3 * NT])
        o_rs = held(late, "o_rs", [P, 3 * NT])
        late_d = ExitStack()
        post_mix_row = held(late_d, "post_mix_row", [P, D])
        pre_mlp_row = held(late_d, "pre_mlp_row", [P, D])
        m_hi, m_lo = w_hi, w_lo
        y_buf = [held(late_d, f"y_buf{s}", [P, D]) for s in range(2)]
        late_d.close()
        big.close()
        post_mlp_row = held(late, "post_mlp_row", [P, D])
        act_ff = late.enter_context(nc.sbuf_tensor("act_ff", [P, FT, HALF], F32, side="right"))
        u_hi, u_lo = w_hi, w_lo
        a_hi = [held(late, f"a_hi{s}", [P, HALF], F32R) for s in range(2)]
        a_lo = [held(late, f"a_lo{s}", [P, HALF], F32R) for s in range(2)]
        down_T = act_ff[:, FT - KT:FT, :]
        final = [act_ff[:, 16 + 2 * s:18 + 2 * s, :].rearrange("p a b -> p (a b)") for s in range(NT // 2)]
        final_sq = act_ff[:, 12:14, :].rearrange("p a b -> p (a b)")

        late_loaded = sem("late_loaded")
        m_turned = sem("m_turned")
        m_hi_ready = sem("m_hi_ready")
        m_lo_ready = sem("m_lo_ready")
        out_done = sem("out_done")
        o_square = sem("o_square")
        o_mean = sem("o_mean")
        o_power = sem("o_power")
        y_done = sem("y_done")
        x_new_ready = sem("x_new_ready")
        h2_normed = sem("h2_normed")
        h2_turned = sem("h2_turned")
        h2_hi_ready = sem("h2_hi_ready")
        h2_lo_ready = sem("h2_lo_ready")
        mlp_hi = sem("mlp_hi")
        mlp_lo = sem("mlp_lo")
        mlp_done = sem("mlp_done")
        relu_done = sem("relu_done")
        square_done = sem("square_done")
        act_hi = sem("act_hi")
        act_lo = sem("act_lo")
        down_act = sem("down_act")
        down_dve = sem("down_dve")
        final_turned = sem("final_turned")
        final_ready = sem("final_ready")
        final_step = sem("final_step")
        final_ready_pool = sem("final_ready_pool")
        out_stored = [sem(f"out_stored{s}") for s in range(NT // 2)]
        HT = NT // 2
        POOL_TILES = (HT, HT + 2)
        STEPS = 2 * FT
        SLOT_LOADS = [loads_before(GDN_HEADS, KT - 2) + NT // 2, loads_before(GDN_HEADS, KT - 1) + NT // 2]
        W_OUT_SPLIT = gemm_block(GDN_HEADS, KT)

        def head_loop_over(eng):
            eng.wait_ge(stored, 32 + 32 * GDN_HEADS)

        def mixed_banks(t):
            return banks(6, 2) if t == 1 else fox_s

        def out_banks(t):
            return banks(2 * (t % 2), 2)

        def final_banks(tt):
            return banks(2 + 2 * (tt % 3), 2)

        block = ctx.enter_context(nc.Block())

        @block.sync
        def _(sp):
            sp.dma_start(x_in[0][:, :], x[0:P, :]).then_inc(x_loaded[0], 16)
            sp.dma_start(pre_row[:, :], pre_mix_norm.rearrange("(a d) -> a d", a=1).to_broadcast([P, D])).then_inc(pre_row_loaded, 16)
            sp.dma_start(const[:, :, :], const_tiles[:, 0:N_CONST * P].rearrange("p (n m) -> p n m", m=P)).then_inc(const_loaded, 16)
            for t in range(1, 4):
                sp.dma_start(x_in[t][:, :], x[t * P:(t + 1) * P, :]).then_inc(x_loaded[t], 16)
            sp.dma_start(causal[:, :], const_tiles[:, N_CONST * P:(N_CONST + 1) * P]).then_inc(params_loaded, 16)
            sp.wait_ge(gate_w_cleared, 1)
            sp.dma_start(w_raw[1][:, :, ROW_CUM:ROW_CUM + FOX_HEADS], w_in_k[:, :, FF:FF + FOX_HEADS]).then_inc(gate_w_loaded, 16)
            sp.dma_start(w_raw[1][:, :, ROW_BETA:ROW_BETA + GDN_HEADS], w_in_k[:, :, GB:GB + GDN_HEADS]).then_inc(gate_w_loaded, 16)
            sp.dma_start(w_raw[1][:, :, ROW_G:ROW_G + GDN_HEADS], w_in_k[:, :, GA:GA + GDN_HEADS]).then_inc(gate_w_loaded, 16)
            def load_block(jn, b, first_col):
                g = gemm_block(jn, b)
                s = slot_of(b)
                before = block_before_in_slot(g, b)
                if not isinstance(before, int) or before >= 0:
                    sp.wait_ge(w_lo_ready, before + 1)
                sp.dma_start(w_raw[s][:, :, :], w_in_k[:, :, bass.ds(first_col + BLOCKS[b], P)]).then_inc(w_loaded[s], 16)

            def load_x(t):
                sp.wait_ge(x_normed, t - 3)
                sp.dma_start(x_in[t % 4][:, :], x[t * P:(t + 1) * P, :]).then_inc(x_loaded[t % 4], 16)

            load_block(0, 0, 0)
            load_x(4)
            load_x(5)
            sp.dma_start(keep[:, :], scan_keep).then_inc(params_loaded, 16)
            sp.wait_ge(params_cleared, 2)
            sp.dma_start(row_bias[ROW_CUM:ROW_CUM + FOX_HEADS, :], fox_f_bias.rearrange("(h a) -> h a", a=1)).then_inc(params_loaded, 16)
            sp.dma_start(row_bias[ROW_G:ROW_G + GDN_HEADS, :], gdn_dt_bias.rearrange("(h a) -> h a", a=1)).then_inc(params_loaded, 16)
            sp.dma_start(row_a[ROW_G:ROW_G + GDN_HEADS, 0:1], gdn_a_log.rearrange("(h a) -> h a", a=1)).then_inc(params_loaded, 16)
            sp.dma_start(conv_rows[:, :], gdn_conv_w.rearrange("t (b c) -> (t b) c", c=P)).then_inc(params_loaded, 16)
            sp.dma_start(fox_norm_row[:, :], fox_out_norm.rearrange("(a d) -> a d", a=1).to_broadcast([P, FOX_DIM])).then_inc(params_loaded, 16)
            sp.dma_start(gdn_norm_row[:, :], gdn_out_norm.rearrange("(a d) -> a d", a=1).to_broadcast([P, GDN_DIM])).then_inc(params_loaded, 16)

            load_x(6)
            load_x(7)
            for b in range(1, NB):
                load_block(0, b, 0)
            sp.wait_ge(gate_dve, GATE_ROWS_DONE)
            sp.dma_start(gate_dram[0:FOX_HEADS, :], gate_rows[ROW_CUM:ROW_CUM + FOX_HEADS, :]).then_inc(stored, 16)
            sp.dma_start(gate_dram[FOX_HEADS:FOX_HEADS + GDN_HEADS, :], gate_rows[ROW_G:ROW_G + GDN_HEADS, :]).then_inc(stored, 16)
            sp.wait_ge(stored, 32)
            first_stage_over(sp)

            def load_g_row(row):
                sp.dma_start(decay[:, :, :].rearrange("p t d -> p (t d)"),
                             gate_dram[bass.ds(row, 1), :].to_broadcast([P, SEQ])).then_inc(g_row_loaded, 16)

            def load_cum_row(row):
                sp.dma_start(cum_row[:, :], gate_dram[bass.ds(row, 1), :].to_broadcast([P, SEQ])).then_inc(cum_row_loaded, 16)

            load_g_row(FOX_HEADS)
            load_cum_row(0)

            def head(j, with_gemm):
                looped = not isinstance(j, int)
                next_g_row = sp.snap(j + (FOX_HEADS + 1)) if looped else 0
                cum_rows = [sp.snap(j * 2 + hh) if looped else j * 2 + hh for hh in (1, 2)]
                mixed_cols = [j * P + P + c for c in (0, D_FOX)]
                def load_w_out(c):
                    g = gemm_block(j + 1, c)
                    sp.wait_ge(w_lo_ready, block_before_in_slot(g, c) + 1)
                    sp.dma_start(w_raw[slot_of(c)][:, :, :], w_out_k[:, :, c * P:(c + 1) * P]).then_inc(w_loaded[slot_of(c)], 16)

                for b in range(NB - 1 if with_gemm else KT - 2):
                    load_block(j + 1, b, j * P + P) if with_gemm else load_w_out(b)
                sp.wait_ge(fox_max, j * NFT + 1 + NT)
                load_cum_row(cum_rows[0])
                if with_gemm:
                    load_block(j + 1, NB - 1, j * P + P)
                else:
                    for c in range(KT - 2, KT):
                        load_w_out(c)
                if with_gemm:
                    sp.wait_ge(dve_prep, (j + 1) * ND + 1)
                    load_g_row(next_g_row)
                    sp.wait_ge(fox_max, j * NFT + (NFT + 1))
                    load_cum_row(cum_rows[1])
                sp.wait_ge(mixed_ready, j * 2 + 2)
                sp.dma_start(mixed[:, bass.ds(mixed_cols[0], P)].rearrange("(t p) c -> p t c", p=P),
                             fox_out[:, :, :, :].rearrange("p t h d -> p t (h d)")).then_inc(stored, 16)
                sp.wait_ge(mixed_ready, j * 2 + 3)
                sp.dma_start(mixed[:, bass.ds(mixed_cols[1], P)].rearrange("(t p) c -> p t c", p=P),
                             u_all).then_inc(stored, 16)

            with sp.Fori(0, GDN_HEADS - 1) as j:
                head(j, True)
            head(GDN_HEADS - 1, False)
            head_loop_over(sp)
            for t in range(NT):
                if t >= 2:
                    sp.wait_ge(m_turned, t - 1)
                s = t % 2
                sp.dma_start(w_raw[s][:, :, :].rearrange("p k m -> p (k m)"), mixed[t * P:(t + 1) * P, P:P + D]).then_inc(w_loaded[s], 16)
                if t == 1:
                    sp.dma_start(post_mix_row[:, :], post_mix_norm.rearrange("(a d) -> a d", a=1).to_broadcast([P, D])).then_inc(late_loaded, 16)
                    sp.dma_start(pre_mlp_row[:, :], pre_mlp_norm.rearrange("(a d) -> a d", a=1).to_broadcast([P, D])).then_inc(late_loaded, 16)
                    sp.dma_start(x_new[:, :, :], x.rearrange("(t p) d -> p t d", p=P)).then_inc(late_loaded, 16)

            def load_up(h, f, s, wait):
                col = sp.snap(f * P) if not isinstance(f, int) else f * P
                if wait:
                    sp.wait_ge(mlp_lo, f + (h * STEPS - 1))
                sp.dma_start(w_raw[s][:, :, :], w_up_k[:, :, bass.ds(col, P)]).then_inc(w_loaded[s], 16)

            def load_down(h, f, s):
                row = sp.snap(f * P)
                sp.wait_ge(mlp_lo, f + (h * STEPS + FT - 1))
                sp.dma_start(w_raw[s][:, :, :].rearrange("p k m -> p (k m)"), w_down[bass.ds(row, P), :]).then_inc(w_loaded[s], 16)

            def store(h, tt):
                t = h * HT + tt
                if t in POOL_TILES:
                    sp.wait_ge(final_ready_pool, POOL_TILES.index(t) + 1)
                else:
                    sp.wait_ge(final_ready, t + 1 - sum(u < t for u in POOL_TILES))
                sp.dma_start(out[t * P:(t + 1) * P, :], final[tt]).then_inc(out_stored[tt], 16)

            for h in range(2):
                for s in range(2):
                    if h == 0:
                        sp.wait_ge(m_turned, NT - 1 + s)
                    load_up(h, s, s, h == 1)
                for f in range(2, 2 * HT):
                    load_up(h, f, f % 2, True)
                    if h == 0 and f == 3:
                        sp.wait_ge(h2_lo_ready, NT)
                        sp.dma_start(post_mlp_row[:, :], post_mlp_norm.rearrange("(a d) -> a d", a=1).to_broadcast([P, D])).then_inc(late_loaded, 16)
                    if h == 1 and f >= HT:
                        store(0, f - HT)
                with sp.Fori(HT, FT // 2) as i:
                    load_up(h, i * 2, 0, True)
                    load_up(h, i * 2 + 1, 1, True)
                with sp.Fori(0, FT // 2) as i:
                    load_down(h, i * 2, 0)
                    load_down(h, i * 2 + 1, 1)
            for tt in range(HT):
                store(1, tt)
            for s in range(HT):
                sp.wait_ge(out_stored[s], 32)

        @block.scalar
        def _(act):
            def unit(u, jn):
                b, n = u // 2, u % 2
                g = gemm_block(jn, b)
                act_out = slice(n * HALF, (n + 1) * HALF)
                src = gemm_ps[:, act_out]
                if b == NB - 1:
                    act.wait_ge(gemm_done, g * 2 + n + 1)
                    for hh in range(2):
                        hr = head_rows(hh)
                        nc.scalar.activation(k_split[hh][hr, act_out], src[hr, :], ACT.Copy).then_inc(k_hi_ready, 1)
                    return
                if u == 0 and (not isinstance(jn, int) or jn > 0):
                    act.wait_ge(k_lo_ready, jn * 4)
                if b in CONV_BLOCKS:
                    idx = 2 * CONV_BLOCKS.index(b) + n
                    if not isinstance(jn, int) or jn * 6 + idx > 0:
                        act.wait_ge(conv_step, (jn * 6 + idx) * TAPS)
                    act.wait_ge(gemm_done, g * 2 + n + 1)
                    halo = zeros[:, :] if n == 0 else taps_in[:, HALF:HALF + TAPS - 1]
                    nc.scalar.activation(taps_in[:, 0:TAPS - 1], halo, ACT.Copy).then_inc(taps_ready, 1)
                    act.wait_ge(taps_ready, jn * 6 + idx + 1)
                    nc.scalar.activation(taps_in[:, TAPS - 1:TAPS - 1 + HALF], src, ACT.Copy).then_inc(gemm_read, 1)
                else:
                    act.wait_ge(gemm_done, g * 2 + n + 1)
                    dst = {0: v_fox[:, act_out], 1: c_raw[:, CZ, act_out], 5: q_fox[:, act_out]}[b]
                    nc.scalar.activation(dst, src, ACT.Copy, scale=FOX_DIM ** -0.5 if b == 5 else 1.0).then_inc(gemm_read, 1)

            def split_hi(jn, b):
                g = gemm_block(jn, b)
                before = block_before_in_slot(g, b)
                act.wait_ge(w_loaded[slot_of(b)], loads_before(jn, b) * 16)
                if not isinstance(before, int) or before >= 0:
                    act.wait_ge(gemm_done, before * 2 + 2)
                nc.scalar.activation(w_hi[slot_of(b)][:, :, :], w_raw[slot_of(b)][:, :, :], ACT.Copy).then_inc(w_hi_ready, 1)

            def x_hi_part(t):
                act.wait_ge(x_turned, t + 1)
                nc.scalar.activation(big_hi[:, :, t * P:(t + 1) * P], banks(2 + 2 * (t % 2), 2).rearrange("p (k m) -> p k m", k=KT),
                                     ACT.Copy).then_inc(x_hi, 1)

            for t in range(NT + 1):
                if t < NT:
                    act.wait_ge(x_loaded[t % 4], 16 * (t // 4 + 1))
                    if t >= 1:
                        act.wait_ge(x_square, t)
                    nc.scalar.activation(x_sq[:, :], x_in[t % 4][:, :], ACT.Square, accum_out=x_ss[:, t:t + 1]).then_inc(x_square, 1)
                if t == NT // 2:
                    act.wait_ge(gate_w_loaded, 48)
                    nc.scalar.activation(w_hi[1][:, :, :], w_raw[1][:, :, :], ACT.Copy).then_inc(w_hi_ready, 1)
                if t >= 2:
                    x_hi_part(t - 2)
            x_hi_part(NT - 1)
            split_hi(0, 0)
            act.wait_ge(params_loaded, PARAM_LOADS * 16)
            for n in range(2):
                act.wait_ge(gemm_done, n + 1)
                nc.scalar.activation(gate_y[:, n * HALF:(n + 1) * HALF], gemm_ps[:, n * HALF:(n + 1) * HALF], ACT.Identity,
                                     bias=row_bias[:, :]).then_inc(gemm_read, 1)
            act.wait_ge(gemm_read, 2)
            nc.scalar.activation(gate_u[:, :], gate_y[:, :], ACT.Abs).then_inc(gate_act, 1)
            split_hi(0, 1)
            act.wait_ge(gate_act, 1)
            nc.scalar.activation(gate_u[:, :], gate_u[:, :], ACT.Exp, scale=-1.0).then_inc(gate_act, 1)
            nc.scalar.activation(row_a[:, 1:2], row_a[:, 0:1], ACT.Exp).then_inc(gate_act, 1)
            act.wait_ge(gate_act, 2)
            nc.scalar.activation(gate_u[:, :], gate_u[:, :], ACT.Ln, bias=1.0).then_inc(gate_act, 1)

            act.wait_ge(half_ready, 2)
            def split_and_unit(u, jn):
                if u % 2 == 0:
                    split_hi(jn, u // 2 + 1)
                unit(u, jn)

            unit(0, 0)
            unit(1, 0)
            split_hi(0, 2)
            act.wait_ge(gate_dve, 4)
            nc.scalar.activation(gate_rows[ROW_BETA:ROW_BETA + GDN_HEADS, :], gate_in[ROW_BETA:ROW_BETA + GDN_HEADS, :], ACT.Exp,
                                 scale=-1.0).then_inc(gate_act, 1)
            unit(2, 0)
            unit(3, 0)
            act.wait_ge(gates_ready, 3)
            for kind, row in ((G_EXP, ROW_G), (G_REST, ROW_REST)):
                nc.scalar.activation(gates_all[:, kind, :, :], turned_gates(row), ACT.Exp).then_inc(gates_ready, 1)
            for u in range(4, 10):
                split_and_unit(u, 0)

            def silu_all(jn):
                act.wait_ge(conv_step, jn * 6 * TAPS + 6 * TAPS)
                act.wait_ge(gemm_read, reads_done(jn, 1, 1))
                nc.scalar.activation(c_raw[:, :, :], c_raw[:, :, :], ACT.Silu).then_inc(silu_done, 1)

            silu_all(0)
            first_stage_over(act)

            def head(j, with_gemm):
                for step in PREP:
                    what, g, lev = step
                    if what in ("out", "split"):
                        ahead, u = PREP_UNITS[g] if g < len(PREP_UNITS) else (1, SCAN_UNITS[0])
                        if what == "out" and (with_gemm or not ahead):
                            unit(u, j + ahead)
                        elif what == "split" and (with_gemm or not ahead):
                            split_hi(j + ahead, u // 2)
                        elif what == "out":
                            w_out_hi(u)
                    elif what == "gl":
                        act.wait_ge(g_row_loaded, j * 16 + 16)
                        act.wait_ge(fox_read, j * NFT + 1)
                        last = decay[:, :, :].rearrange("p t d -> p (t d)")[:, CHUNK - 1::CHUNK]
                        nc.scalar.activation(g_last[:, :], last, ACT.Exp).then_inc(act_prep, 1)
                    elif what == "decay":
                        act.wait_ge(head_gates, j + 1)
                        act.wait_ge(pool_prep, j * NP_ + POOL_PREP[("decay", 0)])
                        for t in range(NT):
                            last = nc.scalar.activation(decay[:, t, :], decay[:, t, :], ACT.Exp, bias=g_head[:, MINUS_G, t:t + 1])
                        last.then_inc(act_prep, 1)
                    elif what in ("k", "q"):
                        act.wait_ge(filled, j * NFILL + FILL[step])
                        if what == "k" and g == 1:
                            act.wait_ge(pool_prep, j * NP_ + POOL_PREP[("kd", 0)])
                        dst = kn if what == "k" else qn
                        nc.scalar.activation(dst[:, :, :], bank4(FILL[step] - 1), ACT.Square).then_inc(act_prep, 1)
                    elif what in ACT_READS:
                        dst = {"fv": v_tok[:, 4 * g:4 * g + 4, :], "z": z_tok[:, 4 * g:4 * g + 4, :],
                               "knT": knT[:, :, :], "qnT": qnT[:, :, :], "kbT": kbT[:, :, :],
                               "qdT": qdT[:, 4 * g:4 * g + 4, :], "X": xb[:, g, :, :], "W": t_inv[:, g, :, :]}[what]
                        act.wait_ge(filled, j * NFILL + FILL[step])
                        if what == "z":
                            act.wait_ge(mixed_ready, j * 2 + 1)
                        if what == "X" and lev == 1:
                            act.wait_ge(stored, j * 32 + 32)
                        nc.scalar.activation(dst, bank4(FILL[step] - 1), ACT.Copy).then_inc(act_prep, 1)

                def p_chunk(i, c):
                    n = FOX_CHUNK[(i, c)]
                    if n % 2 == 1:
                        return
                    nb = min(4, FOX_TILES[i][1] + 1 - 4 * c)
                    act.wait_ge(fox_turned, j * NFC + n + 1)
                    if n >= 2:
                        act.wait_ge(fox_pv, j * NFC + n - 1)
                    nc.scalar.activation(probs_t[0][:, 0:nb, :], fox_t[:, 0:nb * P].rearrange("p (t d) -> p t d", t=nb),
                                         ACT.Copy).then_inc(pt_act, 1)

                def copy_queries(i):
                    hh, qb = FOX_TILES[i]
                    if i >= 2:
                        act.wait_ge(q_ready, j * NFT + i - 1)
                    for rows in (head_rows(hh), head_rows(1 - hh)):
                        last = nc.scalar.activation(q_twice[i % 2][rows, :], q_fox[head_rows(hh), qb * P:(qb + 1) * P], ACT.Copy)
                    last.then_inc(q_copied, 1)

                def fox_square(i):
                    hh, qb = FOX_TILES[i]
                    if i >= 1:
                        act.wait_ge(tail_square, j * (NFT + NT) + i + i // 2)
                    act.wait_ge(fox_read, j * NFT + i + 2)
                    nc.scalar.activation(sq_scratch[:, 0:FOX_DIM], fox_out[:, qb, hh, :], ACT.Square,
                                         accum_out=tail_ss[:, tail_fox(hh) + qb:tail_fox(hh) + qb + 1]).then_inc(tail_square, 1)

                def gdn_square(t):
                    g, tt = divmod(t, 4)
                    if t >= 1:
                        act.wait_ge(tail_square, j * (NFT + NT) + 3 * t - 1)
                    act.wait_ge(o_read, j * NCHUNK + 2 * t + 2)
                    nc.scalar.activation(sq_scratch2[:, :], xb[:, g, tt, :], ACT.Square,
                                         accum_out=tail_ss[:, tail_gdn(g) + tt:tail_gdn(g) + tt + 1]).then_inc(tail_square, 1)

                copy_queries(0)
                for i in range(NCHUNK + 1):
                    if i + 1 < NCHUNK:
                        copy_queries(i + 1)
                    if i >= 2:
                        fox_square(i - 2)
                        if i % 2 == 0:
                            gdn_square(i // 2 - 1)
                    if i >= 1:
                        p_chunk(i - 1, 0)
                    if i < NCHUNK:
                        nk = (FOX_TILES[i][1] + 1) * P
                        act.wait_ge(fox_neg_max, j * NFT + i + 1)
                        nc.scalar.activation(probs[i % 2][:, 0:nk], probs[i % 2][:, 0:nk], ACT.Exp, bias=neg_max[:, i % 2:i % 2 + 1],
                                             accum_out=row_sum[:, i:i + 1]).then_inc(fox_exp, 1)
                        rows, (g, tt) = slice(64 * (i % 2), 64 * (i % 2) + 64), divmod(i // 2, 4)
                        act.wait_ge(scan_o, j * NCHUNK + i + 1)
                        nc.scalar.activation(xb[rows, g, tt, :], scan_b[rows, 0:P], ACT.Copy).then_inc(o_read, 1)
                    if i >= 1 and FOX_TILES[i - 1][1] >= 4:
                        p_chunk(i - 1, 1)
                    if with_gemm and i in SCAN_SPLITS:
                        split_hi(j + 1, SCAN_SPLITS[i])
                    if with_gemm and i in SCAN_OUTS:
                        unit(SCAN_OUTS[i], j + 1)
                    if not with_gemm and i in W_OUT_STEPS:
                        w_out_hi(W_OUT_STEPS[i])
                fox_square(NFT - 1)
                if with_gemm:
                    silu_all(j + 1)

            def w_out_hi(c):
                g = gemm_block(GDN_HEADS, c)
                act.wait_ge(w_loaded[slot_of(c)], loads_before(GDN_HEADS, c) * 16)
                act.wait_ge(gemm_done, 2 * gemm_block(GDN_HEADS, 0))
                nc.scalar.activation(big_hi[:, :, c * P:(c + 1) * P], w_raw[slot_of(c)][:, :, :], ACT.Copy).then_inc(w_hi_ready, 1)

            with act.Fori(0, GDN_HEADS - 1) as j:
                head(j, True)
            head(GDN_HEADS - 1, False)
            head_loop_over(act)

            def m_hi_part(t):
                act.wait_ge(m_turned, t + 1)
                if t >= 2:
                    act.wait_ge(out_done, t - 1)
                nc.scalar.activation(m_hi[t % 2][:, :, :], mixed_banks(t).rearrange("p (k m) -> p k m", k=KT), ACT.Copy).then_inc(m_hi_ready, 1)

            def h2_hi_part(t):
                act.wait_ge(h2_turned, t + 1)
                nc.scalar.activation(h2_hi[:, :, t * P:(t + 1) * P], banks(6, 2).rearrange("p (k m) -> p k m", k=KT), ACT.Copy).then_inc(h2_hi_ready, 1)

            def up_hi(h, f, s):
                act.wait_ge(w_loaded[s], f * 8 + 16 * (h * STEPS // 2 + SLOT_LOADS[s] + 1) - 8 * s)
                if not isinstance(f, int) or h * STEPS + f >= 2:
                    act.wait_ge(mlp_done, f + (h * STEPS - 1))
                else:
                    act.wait_ge(out_done, NT - 1 + f)
                nc.scalar.activation(u_hi[s][:, :, :], w_raw[s][:, :, :], ACT.Copy).then_inc(mlp_hi, 1)

            m_hi_part(0)
            for t in range(NT):
                if t + 1 < NT:
                    m_hi_part(t + 1)
                if t == NT - 1:
                    up_hi(0, 0, 0)
                act.wait_ge(out_done, t + 1)
                if t >= 2:
                    act.wait_ge(h2_turned, t - 1)
                nc.scalar.activation(y_buf[t % 2][:, :], out_banks(t), ACT.Square, accum_out=o_ss[:, t:t + 1]).then_inc(o_square, 1)
                if t >= 1:
                    h2_hi_part(t - 1)
                if t == NT - 1:
                    up_hi(0, 1, 1)
                act.wait_ge(x_new_ready, t + 1)
                nc.scalar.activation(y_buf[t % 2][:, :], x_new[:, t, :], ACT.Square, accum_out=o_ss[:, NT + t:NT + t + 1]).then_inc(o_square, 1)
            def relu(h, f, s):
                act.wait_ge(mlp_done, f + (h * STEPS + 1))
                nc.scalar.activation(act_ff[:, bass.ds(f, 1), :].rearrange("p a t -> p (a t)"), banks(s), ACT.Relu).then_inc(relu_done, 1)

            def down_hi(h, f, s):
                up_hi(h, f + FT, s)
                act.wait_ge(square_done, f + (h * FT + 1))
                nc.scalar.activation(a_hi[s][:, :], act_ff[:, bass.ds(f, 1), :].rearrange("p a t -> p (a t)"), ACT.Copy).then_inc(act_hi, 1)

            def out_of_down(h):
                act.wait_ge(mlp_done, (h + 1) * STEPS)
                for m in range(0, KT, 2):
                    nc.scalar.activation(down_T[:, m, :], banks(m), ACT.Copy).then_inc(down_act, 1)

            def final_square(h, tt):
                t = h * HT + tt
                act.wait_ge(final_turned, t + 1)
                act.wait_ge(o_square, 2 * NT + t)
                nc.scalar.activation(final_sq, final_banks(tt), ACT.Square, accum_out=o_ss[:, 2 * NT + t:2 * NT + t + 1]).then_inc(o_square, 1)

            for h in range(2):
                if h == 1:
                    up_hi(h, 1, 1)
                relu(h, 0, 0)
                for i in range(1, HT // 2 + 1):
                    up_hi(h, i * 2, 0)
                    relu(h, i * 2 - 1, 1)
                    if h == 0 and i == 1:
                        h2_hi_part(NT - 1)
                    if h == 1:
                        final_square(0, 2 * i - 2)
                    up_hi(h, i * 2 + 1, 1)
                    relu(h, i * 2, 0)
                    if h == 1:
                        final_square(0, 2 * i - 1)
                for first_i, last_i in ((HT // 2 + 1, FT // 4), (FT // 4, FT // 2)):
                    if h == 1 and first_i == FT // 4:
                        for s in range(HT):
                            act.wait_ge(out_stored[s], 16)
                    with act.Fori(first_i, last_i) as i:
                        up_hi(h, i * 2, 0)
                        relu(h, i * 2 - 1, 1)
                        up_hi(h, i * 2 + 1, 1)
                        relu(h, i * 2, 0)
                down_hi(h, 0, 0)
                relu(h, FT - 1, 1)
                down_hi(h, 1, 1)
                with act.Fori(1, FT // 2) as i:
                    down_hi(h, i * 2, 0)
                    down_hi(h, i * 2 + 1, 1)
                if h == 0:
                    up_hi(1, 0, 0)
                out_of_down(h)
            for tt in range(HT):
                final_square(1, tt)

        @block.vector
        def _(dve):
            def split_lo(jn, b):
                g = gemm_block(jn, b)
                dve.wait_ge(w_hi_ready, g + 1)
                dve.wait_ge(w_lo_ready, g)
                nc.vector.tensor_tensor(w_lo[slot_of(b)][:, :, :], w_raw[slot_of(b)][:, :, :], w_hi[slot_of(b)][:, :, :].bitcast(F32),
                                        ALU.subtract).then_inc(w_lo_ready, 1)

            def head_taps_copy(jn):
                src = conv_all[:, :].rearrange("p (t k h) -> p t k h", t=TAPS, k=3)[:, :, :, bass.ds(jn, 1)]
                nc.vector.tensor_copy(taps[:, :, :], src.rearrange("p t k h -> p t (k h)")).then_inc(head_taps, 1)

            def unit(u, jn, first_tap=0, last_tap=TAPS - 1):
                b, n = u // 2, u % 2
                if b == NB - 1:
                    cols = slice(n * HALF, (n + 1) * HALF)
                    for hh in range(2):
                        hr, other = head_rows(hh), head_rows(1 - hh)
                        dve.wait_ge(k_hi_ready, (jn * 4 + 2 * n) + hh + 1)
                        step = nc.vector.tensor_tensor(k_split[hh][other, cols], gemm_ps[hr, cols], k_split[hh][hr, cols].bitcast(F32), ALU.subtract)
                        step.then_inc(k_lo_ready, 1)
                    return
                if b not in CONV_BLOCKS:
                    return
                kind = CONV_BLOCKS.index(b)
                done = (jn * 6 + 2 * kind + n) * TAPS
                dst = c_raw[:, kind, n * HALF:(n + 1) * HALF]
                if first_tap == 0:
                    if kind == 0 and n == 0:
                        dve.wait_ge(head_taps, jn + 1)
                    dve.wait_ge(gemm_read, reads_done(jn, b, n))
                    nc.vector.tensor_scalar(dst, taps_in[:, 0:HALF], taps[:, 0, kind:kind + 1], None, ALU.mult).then_inc(conv_step, 1)
                for tap in range(max(first_tap, 1), last_tap + 1):
                    dve.wait_ge(conv_step, done + tap)
                    nc.vector.scalar_tensor_tensor(out=dst, in0=taps_in[:, tap:tap + HALF], scalar=taps[:, tap, kind:kind + 1],
                                                   in1=dst, op0=ALU.mult, op1=ALU.add).then_inc(conv_step, 1)

            def x_lo_part(t):
                dve.wait_ge(x_hi, t + 1)
                cols = slice(t * P, (t + 1) * P)
                nc.vector.tensor_tensor(big_lo[:, :, cols], banks(2 + 2 * (t % 2), 2).rearrange("p (k m) -> p k m", k=KT),
                                        big_hi[:, :, cols].bitcast(F32), ALU.subtract).then_inc(x_lo, 1)

            for t in range(NT):
                dve.wait_ge(x_square, t + 1)
                nc.vector.tensor_scalar(x_ms[:, t:t + 1], x_ss[:, t:t + 1], 1.0 / D, EPS, ALU.mult, ALU.add).then_inc(x_mean, 1)
                if t >= 2:
                    x_lo_part(t - 2)
                if t == 0:
                    dve.wait_ge(pre_row_loaded, 16)
                if t >= 2:
                    dve.wait_ge(x_turned, t - 1)
                dve.wait_ge(x_power, t + 1)
                nc.vector.scalar_tensor_tensor(out=x_n[t % 2][:, :], in0=x_in[t % 4][:, :], scalar=x_rs[:, t:t + 1], in1=pre_row[:, :],
                                               op0=ALU.mult, op1=ALU.mult).then_inc(x_normed, 1)
                if t == NT // 2:
                    dve.wait_ge(w_hi_ready, 1)
                    nc.vector.tensor_tensor(w_lo[1][:, :, :], w_raw[1][:, :, :], w_hi[1][:, :, :].bitcast(F32), ALU.subtract).then_inc(w_lo_ready, 1)
            x_lo_part(NT - 2)
            x_lo_part(NT - 1)
            split_lo(0, 0)
            dve.wait_ge(const_loaded, 16)
            dve.wait_ge(params_loaded, PARAM_LOADS * 16)
            nc.vector.tensor_copy(ident_bf[:, :], ident).then_inc(dve_prep, 1)
            nc.vector.tensor_copy(causal_bf[:, :], causal[:, :]).then_inc(fox_max, 1)
            nc.vector.memset(taps_in[:, 0:TAPS - 1], 0.0).then_inc(fox_read, 1)
            nc.vector.memset(wait_holder[:, :], 0.0).then_inc(mixed_ready, 1)
            log_rows = slice(ROW_CUM, ROW_BETA + GDN_HEADS)
            g_rows = slice(ROW_G, ROW_G + GDN_HEADS)
            r_rows = slice(ROW_REST, ROW_REST + GDN_HEADS)
            split_lo(0, 1)
            dve.wait_ge(gate_act, 4)
            dve.wait_ge(gate_pool, 1)
            nc.vector.scalar_tensor_tensor(out=gate_in[log_rows, :], in0=gate_y[log_rows, :], scalar=0.0, in1=gate_u[log_rows, :],
                                           op0=ALU.min, op1=ALU.subtract, reverse1=True).then_inc(gate_dve, 1)
            nc.vector.scalar_tensor_tensor(out=gate_in[g_rows, :], in0=gate_y[g_rows, :], scalar=0.0, in1=gate_u[g_rows, :],
                                           op0=ALU.max, op1=ALU.add).then_inc(gate_dve, 1)
            dve.wait_ge(gate_dve, 2)
            nc.vector.tensor_scalar(gate_in[g_rows, :], gate_in[g_rows, :], row_a[g_rows, 1:2], -1.0, ALU.mult, ALU.mult).then_inc(gate_dve, 1)
            dve.wait_ge(gate_dve, 3)
            nc.vector.tensor_tensor_scan(gate_rows[:, :], keep[:, :], gate_in[:, :], 0.0, ALU.mult, ALU.add).then_inc(gate_dve, 1)
            dve.wait_ge(gate_dve, 4)
            by_chunk = gate_rows[g_rows, :].rearrange("p (n c) -> p n c", c=CHUNK)
            nc.vector.tensor_tensor(gate_rows[r_rows, :].rearrange("p (n c) -> p n c", c=CHUNK),
                                    by_chunk[:, :, CHUNK - 1:CHUNK].to_broadcast([GDN_HEADS, NCHUNK, CHUNK]), by_chunk,
                                    ALU.subtract).then_inc(gate_dve, 1)
            dve.wait_ge(gate_turned, 1)
            nc.vector.tensor_copy(conv_all[:, :], fox_t[:, 0:TAPS * 3 * GDN_HEADS]).then_inc(gates_ready, 1)
            dve.wait_ge(gates_ready, 1)
            head_taps_copy(0)
            def split_and_unit(u, jn):
                if u % 2 == 0:
                    split_lo(jn, u // 2 + 1)
                unit(u, jn)

            split_lo(0, 2)
            dve.wait_ge(gate_turned, 2)
            nc.vector.tensor_copy(gates_all[:, BETA, :, :], turned_gates(ROW_BETA)).then_inc(gates_ready, 1)
            nc.vector.tensor_scalar(gates_all[:, MINUS_G, :, :], turned_gates(ROW_G), -1.0, None, ALU.mult).then_inc(gates_ready, 1)
            for u in range(4, 10):
                split_and_unit(u, 0)
            first_stage_over(dve)

            def head(j, with_gemm):
                nc.vector.tensor_copy(g_head[:, :, :], gates_all[:, :, bass.ds(j, 1), :].rearrange("p k h t -> p k (h t)")).then_inc(head_gates, 1)
                if with_gemm:
                    dve.wait_ge(conv_step, j * 6 * TAPS + 6 * TAPS)
                    head_taps_copy(j + 1)
                dve.wait_ge(head_gates, j + 1)
                for step in PREP:
                    what, g, lev = step
                    if what in ("out", "split"):
                        ahead, u = PREP_UNITS[g] if g < len(PREP_UNITS) else (1, SCAN_UNITS[0])
                        if what == "out" and (with_gemm or not ahead):
                            unit(u, j + ahead)
                        elif what == "split" and (with_gemm or not ahead):
                            split_lo(j + ahead, u // 2)
                        elif what == "out":
                            w_out_lo(u)
                        continue
                    if what not in DVE_READS:
                        continue
                    src = bank4(FILL[step] - 1)
                    four = slice(4 * g, 4 * g + 4)
                    if what in ("k", "q"):
                        side = 0 if what == "k" else 1
                        dst = kn if what == "k" else qn
                        dve.wait_ge(act_prep, j * NA + ACT_PREP[("square", what, g)])
                        nc.vector.tensor_reduce(sums[:, side, :], dst[:, :, :], AX_X, ALU.add).then_inc(norm_sum, 1)
                        dve.wait_ge(norm_sum, j * 4 + 2 * g + side + 1)
                        nc.vector.tensor_scalar(means[:, side, :], sums[:, side, :], EPS, None, ALU.add).then_inc(dve_prep, 1)
                        if what == "q":
                            dve.wait_ge(dve_prep, j * ND + 1 + DVE_PREP[("k", g, 0)])
                            nc.vector.tensor_tensor(kbg[:, g, :, :], kn[:, :, :], wide(g_head[:, BETA, four], P), ALU.mult).then_inc(dve_prep, 1)
                        dve.wait_ge(pool_prep, j * NP_ + POOL_PREP[("power", what, g)])
                        nc.vector.scalar_tensor_tensor(out=dst[:, :, :], in0=src, scalar=1.0 if what == "k" else GDN_DIM ** -0.5,
                                                       in1=wide(powers[:, side, :], P), op0=ALU.mult, op1=ALU.mult).then_inc(dve_prep, 1)
                        continue
                    dve.wait_ge(filled, j * NFILL + FILL[step])
                    if what == "v":
                        nc.vector.tensor_tensor(vb[:, g, :, :], src, wide(g_head[:, BETA, four], P), ALU.mult).then_inc(dve_prep, 1)
                    elif what in ("N", "A"):
                        dve.wait_ge(act_prep, j * NA + ACT_PREP[("decay", 0, 0)])
                        dst = n_low[:, g, :, :] if what == "N" else a_t[:, four, :]
                        nc.vector.tensor_tensor(dst, src, decay[:, four, :], ALU.mult).then_inc(dve_prep, 1)
                    elif what == "M0":
                        nc.vector.tensor_tensor(t_inv[:, g, :, :], stacked(ident, 4), src, ALU.subtract).then_inc(dve_prep, 1)
                    elif what == "TX":
                        nc.vector.tensor_tensor(t_inv[:, g, :, :], t_inv[:, g, :, :], src, ALU.subtract).then_inc(dve_prep, 1)
                    elif what == "XR":
                        nc.vector.tensor_tensor(r_inv[:, g, :, :], r_inv[:, g, :, :], src, ALU.subtract).then_inc(dve_prep, 1)
                    elif what == "U":
                        nc.vector.tensor_copy(xb[:, g, :, :], src).then_inc(dve_prep, 1)

                def p_chunk(i, c):
                    n = FOX_CHUNK[(i, c)]
                    if n % 2 == 0:
                        return
                    nb = min(4, FOX_TILES[i][1] + 1 - 4 * c)
                    dve.wait_ge(fox_turned, j * NFC + n + 1)
                    if n >= 2:
                        dve.wait_ge(fox_pv, j * NFC + n - 1)
                    nc.vector.tensor_copy(probs_t[1][:, 0:nb, :], fox_t[:, 0:nb * P].rearrange("p (t d) -> p t d", t=nb)).then_inc(pt_dve, 1)

                def tail_means(h):
                    f, g = slice(tail_fox(h), tail_fox(h) + NT), slice(tail_gdn(h), tail_gdn(h) + NT // 2)
                    dve.wait_ge(tail_square, j * (NFT + NT) + TAIL_SQUARES[h])
                    nc.vector.tensor_scalar(tail_ms[:, f], tail_ss[:, f], 1.0 / FOX_DIM, EPS, ALU.mult, ALU.add).then_inc(tail_dve, 1)
                    nc.vector.tensor_scalar(tail_ms[:, g], tail_ss[:, g], 1.0 / GDN_DIM, EPS, ALU.mult, ALU.add).then_inc(tail_dve, 1)

                def tail_norm(h):
                    t0 = j * 10 + 6 * h
                    fo, u, z = fox_out[:, :, h, :], xb[:, h, :, :], z_tok[:, 4 * h:4 * h + 4, :]
                    dve.wait_ge(tail_power, j * 2 + h + 1)
                    nc.vector.tensor_tensor(fo, fo, wide(tail_rs[:, tail_fox(h):tail_fox(h) + NT], FOX_DIM), ALU.mult).then_inc(tail_dve, 1)
                    nc.vector.tensor_tensor(u, u, wide(tail_rs[:, tail_gdn(h):tail_gdn(h) + NT // 2], GDN_DIM), ALU.mult).then_inc(tail_dve, 1)
                    dve.wait_ge(tail_dve, t0 + 3)
                    done = mixed_ready if h == 1 else tail_dve
                    nc.vector.tensor_tensor(fo, fo, stacked(fox_norm_row[:, :], NT), ALU.mult).then_inc(done, 1)
                    dve.wait_ge(z_normed, j + 1)
                    dve.wait_ge(tail_dve, t0 + 4)
                    nc.vector.tensor_tensor(u, u, z, ALU.mult).then_inc(done, 1)

                nc.vector.memset(state[:, :], 0.0).then_inc(state_ready, 1)
                for i in range(NCHUNK + 1):
                    if i < NCHUNK:
                        rows, (g, tt) = slice(64 * (i % 2), 64 * (i % 2) + 64), divmod(i // 2, 4)
                        dve.wait_ge(scan_v, j * NCHUNK + i + 1)
                        nc.vector.tensor_tensor(v_new[rows, :], xb[rows, g, tt, :], scan_a[rows, 0:P], ALU.subtract).then_inc(v_new_ready, 1)
                        nk = (FOX_TILES[i][1] + 1) * P
                        dve.wait_ge(fox_scored, j * NFT + i + 1)
                        if i == 0 or i == NT:
                            dve.wait_ge(cum_row_loaded, j * 32 + 16 * (i // NT + 1))
                        if i >= 2:
                            dve.wait_ge(fox_pv, j * NFC + FOX_CHUNK[(i - 2, FOX_TILES[i - 2][1] // 4)] + 1)
                        nc.vector.memset(wait_holder[:, :], 0.0)
                        nc.vector.tensor_tensor_reduce(out=probs[i % 2][:, 0:nk], in0=fox_s[:, 0:nk], in1=cum_row[:, 0:nk], scale=1.0,
                                                       scalar=LOWEST, op0=ALU.add, op1=ALU.max,
                                                       accum_out=row_max[:, i % 2:i % 2 + 1]).then_inc(fox_max, 1)
                        dve.wait_ge(fox_max, j * NFT + i + 2)
                        nc.vector.tensor_scalar(neg_max[:, i % 2:i % 2 + 1], row_max[:, i % 2:i % 2 + 1], -1.0, None, ALU.mult).then_inc(fox_neg_max, 1)
                        dve.wait_ge(scan_s, j * NCHUNK + i + 1)
                        nc.vector.scalar_tensor_tensor(out=state[:, :], in0=state[:, :], scalar=g_last[:, i:i + 1], in1=scan_a[:, P:2 * P],
                                                       op0=ALU.mult, op1=ALU.add).then_inc(state_ready, 1)
                    if i >= 1:
                        hh, qb = FOX_TILES[i - 1]
                        p_chunk(i - 1, 0)
                        if qb >= 4:
                            p_chunk(i - 1, 1)
                        dve.wait_ge(fox_exp, j * NFT + i)
                        nc.vector.reciprocal(row_inv[:, i - 1:i], row_sum[:, i - 1:i]).then_inc(fox_inv, 1)
                        if i == 1:
                            dve.wait_ge(stored, j * 32 + 32)
                        dve.wait_ge(fox_inv, j * NFT + i)
                        dve.wait_ge(fox_pv, j * NFC + FOX_CHUNK[(i - 1, qb // 4)] + 1)
                        nc.vector.tensor_scalar(fox_out[:, qb, hh, :], fox_o[:, 0:FOX_DIM], row_inv[:, i - 1:i], None, ALU.mult).then_inc(fox_read, 1)
                    if i == MEANS_STEP:
                        tail_means(0)
                    if i == MEANS_STEP + 1:
                        tail_norm(0)
                    if with_gemm and i in SCAN_OUTS:
                        unit(SCAN_OUTS[i], j + 1, 0, 1)
                    if with_gemm and i - 1 in SCAN_OUTS:
                        unit(SCAN_OUTS[i - 1], j + 1, 2, 3)
                tail_means(1)
                tail_norm(1)

            def w_out_lo(c):
                g = gemm_block(GDN_HEADS, c)
                dve.wait_ge(w_hi_ready, g + 1)
                dve.wait_ge(w_lo_ready, g)
                cols = slice(c * P, (c + 1) * P)
                nc.vector.tensor_tensor(big_lo[:, :, cols], w_raw[slot_of(c)][:, :, :], big_hi[:, :, cols].bitcast(F32), ALU.subtract).then_inc(w_lo_ready, 1)

            with dve.Fori(0, GDN_HEADS - 1) as j:
                head(j, True)
            head(GDN_HEADS - 1, False)
            head_loop_over(dve)

            def m_lo_part(t):
                dve.wait_ge(m_hi_ready, t + 1)
                nc.vector.tensor_tensor(m_lo[t % 2][:, :, :], mixed_banks(t).rearrange("p (k m) -> p k m", k=KT), m_hi[t % 2][:, :, :].bitcast(F32),
                                        ALU.subtract).then_inc(m_lo_ready, 1)

            def h2_lo_part(t):
                dve.wait_ge(h2_hi_ready, t + 1)
                cols = slice(t * P, (t + 1) * P)
                nc.vector.tensor_tensor(h2_lo[:, :, cols], banks(6, 2).rearrange("p (k m) -> p k m", k=KT), h2_hi[:, :, cols].bitcast(F32),
                                        ALU.subtract).then_inc(h2_lo_ready, 1)

            def up_lo(h, f, s):
                dve.wait_ge(mlp_hi, f + (h * STEPS + 1))
                nc.vector.tensor_tensor(u_lo[s][:, :, :], w_raw[s][:, :, :], u_hi[s][:, :, :].bitcast(F32), ALU.subtract).then_inc(mlp_lo, 1)

            m_lo_part(0)
            for t in range(NT):
                if t + 1 < NT:
                    m_lo_part(t + 1)
                if t == NT - 1:
                    up_lo(0, 0, 0)
                y = y_buf[t % 2][:, :]
                dve.wait_ge(o_square, 2 * t + 1)
                nc.vector.tensor_scalar(o_ms[:, t:t + 1], o_ss[:, t:t + 1], 1.0 / D, EPS, ALU.mult, ALU.add).then_inc(o_mean, 1)
                if t >= 1:
                    h2_lo_part(t - 1)
                if t == NT - 1:
                    up_lo(0, 1, 1)
                if t == 0:
                    dve.wait_ge(late_loaded, 48)
                dve.wait_ge(o_power, 2 * t + 1)
                nc.vector.scalar_tensor_tensor(out=y, in0=out_banks(t), scalar=o_rs[:, t:t + 1], in1=post_mix_row[:, :],
                                               op0=ALU.mult, op1=ALU.mult).then_inc(y_done, 1)
                dve.wait_ge(y_done, t + 1)
                nc.vector.tensor_tensor(x_new[:, t, :], x_new[:, t, :], y, ALU.add).then_inc(x_new_ready, 1)
                dve.wait_ge(o_square, 2 * t + 2)
                nc.vector.tensor_scalar(o_ms[:, NT + t:NT + t + 1], o_ss[:, NT + t:NT + t + 1], 1.0 / D, EPS, ALU.mult, ALU.add).then_inc(o_mean, 1)
                dve.wait_ge(o_power, 2 * t + 2)
                nc.vector.scalar_tensor_tensor(out=y, in0=x_new[:, t, :], scalar=o_rs[:, NT + t:NT + t + 1], in1=pre_mlp_row[:, :],
                                               op0=ALU.mult, op1=ALU.mult).then_inc(h2_normed, 1)
            def square(h, f, s):
                a = act_ff[:, bass.ds(f, 1), :].rearrange("p a t -> p (a t)")
                dve.wait_ge(relu_done, f + (h * FT + 1))
                nc.vector.tensor_tensor(a, a, a, ALU.mult).then_inc(square_done, 1)

            def down_lo(h, f, s):
                up_lo(h, f + FT, s)
                dve.wait_ge(act_hi, f + (h * FT + 1))
                nc.vector.tensor_tensor(a_lo[s][:, :], act_ff[:, bass.ds(f, 1), :].rearrange("p a t -> p (a t)"), a_hi[s][:, :].bitcast(F32),
                                        ALU.subtract).then_inc(act_lo, 1)

            def out_of_down(h):
                dve.wait_ge(mlp_done, (h + 1) * STEPS)
                for m in range(1, KT, 2):
                    nc.vector.tensor_copy(down_T[:, m, :], banks(m)).then_inc(down_dve, 1)

            def final_mean(h, tt):
                t = h * HT + tt
                dve.wait_ge(o_square, 2 * NT + t + 1)
                nc.vector.tensor_scalar(o_ms[:, 2 * NT + t:2 * NT + t + 1], o_ss[:, 2 * NT + t:2 * NT + t + 1], 1.0 / D, EPS, ALU.mult, ALU.add).then_inc(o_mean, 1)

            def finish(h, tt):
                t = h * HT + tt
                dve.wait_ge(late_loaded, 64)
                dve.wait_ge(o_power, 2 * NT + t + 1)
                if h == 1:
                    dve.wait_ge(out_stored[tt], 16)
                nc.vector.scalar_tensor_tensor(out=final[tt], in0=final_banks(tt), scalar=o_rs[:, 2 * NT + t:2 * NT + t + 1],
                                               in1=post_mlp_row[:, :], op0=ALU.mult, op1=ALU.mult).then_inc(final_step, 1)
                if t not in POOL_TILES:
                    dve.wait_ge(final_step, t + 1)
                    nc.vector.tensor_tensor(final[tt], final[tt], x_new[:, t, :], ALU.add).then_inc(final_ready, 1)

            for h in range(2):
                if h == 1:
                    up_lo(h, 1, 1)
                square(h, 0, 0)
                for i in range(1, HT // 2 + 1):
                    up_lo(h, i * 2, 0)
                    square(h, i * 2 - 1, 1)
                    if h == 0 and i == 1:
                        h2_lo_part(NT - 1)
                    if h == 1:
                        final_mean(0, 2 * i - 2)
                        finish(0, 2 * i - 2)
                    up_lo(h, i * 2 + 1, 1)
                    square(h, i * 2, 0)
                    if h == 1:
                        final_mean(0, 2 * i - 1)
                        finish(0, 2 * i - 1)
                with dve.Fori(HT // 2 + 1, FT // 2) as i:
                    up_lo(h, i * 2, 0)
                    square(h, i * 2 - 1, 1)
                    up_lo(h, i * 2 + 1, 1)
                    square(h, i * 2, 0)
                down_lo(h, 0, 0)
                square(h, FT - 1, 1)
                down_lo(h, 1, 1)
                with dve.Fori(1, FT // 2) as i:
                    down_lo(h, i * 2, 0)
                    down_lo(h, i * 2 + 1, 1)
                if h == 0:
                    up_lo(1, 0, 0)
                out_of_down(h)
            final_mean(1, 0)
            for tt in range(HT):
                if tt + 1 < HT:
                    final_mean(1, tt + 1)
                finish(1, tt)

        @block.gpsimd
        def _(pool):
            nc.gpsimd.memset(w_raw[1][:, :, :], 0.0).then_inc(gate_w_cleared, 1)
            nc.gpsimd.memset(row_bias[:, :], 0.0).then_inc(params_cleared, 1)
            nc.gpsimd.memset(row_a[:, :], 0.0).then_inc(params_cleared, 1)
            nc.gpsimd.memset(zeros[:, :], 0.0).then_inc(half_ready, 1)
            nc.gpsimd.memset(minus_half[:, :], -0.5).then_inc(half_ready, 1)
            nc.gpsimd.memset(gate_in[:, :], 0.0).then_inc(gate_pool, 1)
            pool.wait_ge(half_ready, 2)
            for t in range(NT):
                pool.wait_ge(x_mean, t + 1)
                nc.gpsimd.tensor_tensor(x_rs[:, t:t + 1], x_ms[:, t:t + 1], minus_half[:, 0:1], ALU.pow).then_inc(x_power, 1)
            first_stage_over(pool)

            def head(j, with_gemm):
                base = j * NP_
                pool.wait_ge(head_gates, j + 1)
                for step in PREP:
                    what, g, lev = step
                    four = slice(4 * g, 4 * g + 4)
                    if what in ("k", "q"):
                        side = 0 if what == "k" else 1
                        pool.wait_ge(dve_prep, j * ND + 1 + DVE_PREP[("mean", what, g)])
                        nc.gpsimd.tensor_tensor(powers[:, side, :], means[:, side, :], minus_half[:, 0:4], ALU.pow).then_inc(pool_prep, 1)
                    elif what == "gl":
                        pool.wait_ge(act_prep, j * NA + ACT_PREP[("gl", 0, 0)])
                        nc.gpsimd.tensor_tensor(decay[:, :, :], decay[:, :, :], stacked(const[:, DECAY_MASK, :], NT), ALU.add).then_inc(pool_prep, 1)
                    elif what == "knT":
                        pool.wait_ge(dve_prep, j * ND + 1 + DVE_PREP[("k", g, 0)])
                        nc.gpsimd.tensor_tensor(kd[:, four, :], kn[:, :, :], wide(g_head[:, G_REST, four], P), ALU.mult).then_inc(pool_prep, 1)
                    elif what == "kbT":
                        pool.wait_ge(filled, j * NFILL + FILL[step])
                        nc.gpsimd.tensor_tensor(kbg[:, g, :, :], kbg[:, g, :, :], wide(g_head[:, G_EXP, four], P), ALU.mult).then_inc(pool_prep, 1)
                    elif what == "qnT":
                        pool.wait_ge(filled, j * NFILL + FILL[step])
                        nc.gpsimd.tensor_tensor(qn[:, :, :], qn[:, :, :], wide(g_head[:, G_EXP, four], P), ALU.mult).then_inc(pool_prep, 1)
                    elif what == "N":
                        pool.wait_ge(dve_prep, j * ND + 1 + DVE_PREP[step])
                        level(j, g, 0)
                        pool.wait_ge(pool_prep, base + POOL_PREP[("level", g, 0)])
                        nc.gpsimd.tensor_tensor(r_inv[:, g, :, :], stacked(ident, 4), n_lev[:, g, :, :], ALU.subtract).then_inc(pool_prep, 1)
                    elif what == "M0":
                        pool.wait_ge(filled, j * NFILL + FILL[step])
                        pool.wait_ge(pool_prep, base + POOL_PREP[("R0", g)])
                        level(j, g, 1)
                    elif what == "X" and lev < LEVELS - 1:
                        pool.wait_ge(filled, j * NFILL + FILL[step])
                        level(j, g, lev + 1)
                for i in range(NFT):
                    pool.wait_ge(q_copied, j * NFT + i + 1)
                    if i >= 2:
                        pool.wait_ge(fox_scored, j * NFT + i - 1)
                    nc.gpsimd.tensor_tensor(q_hi[i % 2][:, :], q_twice[i % 2][:, :], zeros[:, 0:1].to_broadcast([P, P]), ALU.add).then_inc(q_hi_ready, 1)
                    pool.wait_ge(q_hi_ready, j * NFT + i + 1)
                    nc.gpsimd.tensor_tensor(q_lo[i % 2][:, :], q_twice[i % 2][:, :], q_hi[i % 2][:, :].bitcast(F32), ALU.subtract).then_inc(q_ready, 1)
                    if with_gemm and i - 1 in SCAN_SPLITS:
                        split_lo(j + 1, SCAN_SPLITS[i - 1])
                    if not with_gemm and i - 1 in W_OUT_STEPS:
                        w_out_lo(W_OUT_STEPS[i - 1])
                    if i == Z_STEP:
                        nc.gpsimd.tensor_tensor(z_tok[:, :, :], z_tok[:, :, :], stacked(gdn_norm_row[:, :], NT), ALU.mult).then_inc(z_normed, 1)
                    if i == MEANS_STEP + 1:
                        tail_powers(j, 0)
                tail_powers(j, 1)

            def tail_powers(j, h):
                cols = slice(h * TAIL_HALF, (h + 1) * TAIL_HALF)
                pool.wait_ge(tail_dve, j * 10 + (6 * h + 2))
                nc.gpsimd.tensor_tensor(tail_rs[:, cols], tail_ms[:, cols], minus_half[:, 0:TAIL_HALF], ALU.pow).then_inc(tail_power, 1)

            def level(j, g, lev):
                nc.gpsimd.tensor_tensor(n_lev[:, g, :, :], n_low[:, g, :, :], stacked(const[:, LEVEL_MASK + lev, :], 4), ALU.mult).then_inc(pool_prep, 1)

            def split_lo(jn, b):
                g = gemm_block(jn, b)
                pool.wait_ge(w_hi_ready, g + 1)
                pool.wait_ge(w_lo_ready, g)
                nc.gpsimd.tensor_tensor(w_lo[slot_of(b)][:, :, :], w_raw[slot_of(b)][:, :, :], w_hi[slot_of(b)][:, :, :].bitcast(F32),
                                        ALU.subtract).then_inc(w_lo_ready, 1)

            def w_out_lo(c):
                g = gemm_block(GDN_HEADS, c)
                cols = slice(c * P, (c + 1) * P)
                pool.wait_ge(w_hi_ready, g + 1)
                pool.wait_ge(w_lo_ready, g)
                nc.gpsimd.tensor_tensor(big_lo[:, :, cols], w_raw[slot_of(c)][:, :, :], big_hi[:, :, cols].bitcast(F32),
                                        ALU.subtract).then_inc(w_lo_ready, 1)

            with pool.Fori(0, GDN_HEADS - 1) as j:
                head(j, True)
            head(GDN_HEADS - 1, False)
            head_loop_over(pool)
            nc.gpsimd.memset(halves[:, :], -0.5).then_inc(half_ready, 1)
            pool.wait_ge(half_ready, 3)
            for n in range(3 * NT):
                col = (n // 2 + NT * (n % 2)) if n < 2 * NT else n
                pool.wait_ge(o_mean, n + 1)
                nc.gpsimd.tensor_tensor(o_rs[:, col:col + 1], o_ms[:, col:col + 1], halves[:, 0:1], ALU.pow).then_inc(o_power, 1)
                t = n - 2 * NT - 1
                if t in POOL_TILES:
                    pool.wait_ge(final_step, t + 1)
                    nc.gpsimd.tensor_tensor(final[t - HT], final[t - HT], x_new[:, t, :], ALU.add).then_inc(final_ready_pool, 1)

        @block.tensor
        def _(pe):
            def unit_part(s, n, k):
                rhs_hi = big_hi[:, k, n * HALF:(n + 1) * HALF]
                rhs_lo = big_lo[:, k, n * HALF:(n + 1) * HALF]
                acc = banks(n)
                nc.tensor.matmul(acc, w_hi[s][:, k, :], rhs_hi, start=(k == 0), stop=False)
                nc.tensor.matmul(acc, w_hi[s][:, k, :], rhs_lo, start=False, stop=False)
                last = nc.tensor.matmul(acc, w_lo[s][:, k, :], rhs_hi, start=False, stop=(k == KT - 1))
                if k == KT - 1:
                    last.then_inc(gemm_done, 1)

            def half_block_out(jn, b, n):
                if b > 0:
                    pe.wait_ge(gemm_read, reads_done(jn, b - 1, n))
                elif isinstance(jn, int) and jn == 0:
                    pe.wait_ge(gemm_read, n + 1)
                else:
                    pe.wait_ge(k_lo_ready, jn * 4 - 2 + 2 * n)

            def unit(u, jn):
                for k in range(KT):
                    part(u, jn, k)

            def part(u, jn, k):
                b, n = u // 2, u % 2
                if k == 0:
                    if n == 0:
                        pe.wait_ge(w_lo_ready, gemm_block(jn, b) + 1)
                    half_block_out(jn, b, n)
                unit_part(slot_of(b), n, k)

            pe.wait_ge(const_loaded, 16)
            for t in range(NT):
                pe.wait_ge(x_normed, t + 1)
                if t >= 2:
                    pe.wait_ge(x_lo, t - 1)
                for k in range(KT):
                    last = nc.tensor.transpose(banks(2 + 2 * (t % 2), 2)[:, k * P:(k + 1) * P], x_n[t % 2][:, k * P:(k + 1) * P], ident)
                last.then_inc(x_turned, 1)
            pe.wait_ge(x_lo, NT)
            pe.wait_ge(w_lo_ready, 1)
            pe.wait_ge(params_loaded, PARAM_LOADS * 16)
            nc.tensor.transpose(fox_t[:, 0:TAPS * 3 * GDN_HEADS], conv_rows[:, :], ident[0:TAPS * 3 * GDN_HEADS, 0:TAPS * 3 * GDN_HEADS]).then_inc(gate_turned, 1)
            for n in range(2):
                for k in range(KT):
                    unit_part(1, n, k)
            for u in range(4):
                unit(u, 0)
            pe.wait_ge(gate_dve, GATE_ROWS_DONE)
            pe.wait_ge(gate_act, 5)
            for t in range(NT):
                last = nc.tensor.transpose(banks(2, 2)[:, t * P:(t + 1) * P], gate_rows[:, t * P:(t + 1) * P], ident)
            last.then_inc(gate_turned, 1)
            for u in range(4, 10):
                unit(u, 0)
            first_stage_over(pe)

            def four_products(f, lhs, rhs):
                for i in range(4):
                    last = nc.tensor.matmul(bank(f)[:, i * P:(i + 1) * P], lhs(i), rhs(i), start=True, stop=True)
                last.then_inc(filled, 1)

            def four_turned(f, src):
                for i in range(4):
                    last = nc.tensor.transpose(bank(f)[:, i * P:(i + 1) * P], src(i), ident)
                last.then_inc(filled, 1)

            def head(j, with_gemm):
                pe.wait_ge(fox_read, j * NFT + 1)

                def after_act(name):
                    pe.wait_ge(act_prep, j * NA + ACT_PREP[name])

                def after_dve(name):
                    pe.wait_ge(dve_prep, j * ND + 1 + DVE_PREP[name])

                def after_pool(name):
                    pe.wait_ge(pool_prep, j * NP_ + POOL_PREP[name])

                for step in PREP:
                    what, g, lev = step
                    if what == "part":
                        unit_index, k = divmod(g, KT)
                        ahead, u = PREP_UNITS[unit_index]
                        if with_gemm or not ahead:
                            part(u, j + ahead, k)
                        continue
                    if what in ("gl", "decay", "out", "split"):
                        continue
                    if step == ("k", 0, 0):
                        pe.wait_ge(silu_done, j + 1)
                    f = FILL[step] - 1
                    if f >= NFILL_BANKS:
                        old = FILLS[f - NFILL_BANKS]
                        (after_act if old[0] in ACT_READS else after_dve)(old)
                    tok = [slice((4 * g + i) * P, (4 * g + i + 1) * P) for i in range(4)]
                    if what == "fv":
                        four_turned(f, lambda i: v_fox[:, tok[i]])
                    elif what in ("z", "k", "q", "v"):
                        kind = {"z": CZ, "k": CK, "q": CQ, "v": CV}[what]
                        four_turned(f, lambda i: c_raw[:, kind, tok[i]])
                    elif what == "knT":
                        after_dve(("k", g, 0))
                        four_turned(f, lambda i: kn[:, i, :])
                    elif what == "qnT":
                        after_dve(("q", g, 0))
                        four_turned(f, lambda i: qn[:, i, :])
                    elif what == "qdT":
                        after_pool(("qd", g))
                        four_turned(f, lambda i: qn[:, i, :])
                    elif what == "kbT":
                        after_dve(("kb", g))
                        four_turned(f, lambda i: kbg[:, g, i, :])
                    elif what == "N":
                        after_act(("kbT", g, 0))
                        four_products(f, lambda i: knT[:, i, :], lambda i: kbT[:, i, :])
                    elif what == "A":
                        after_act(("qnT", g, 0))
                        four_products(f, lambda i: knT[:, i, :], lambda i: qnT[:, i, :])
                    elif what == "M0":
                        after_pool(("level", g, 0))
                        four_turned(f, lambda i: n_lev[:, g, i, :])
                    elif what == "X":
                        after_pool(("level", g, lev))
                        after_dve(("TX", g, lev - 1) if lev > 1 else ("M0", g, 0))
                        four_products(f, lambda i: n_lev[:, g, i, :], lambda i: t_inv[:, g, i, :])
                    elif what == "TX":
                        after_act(("X", g, lev))
                        if lev > 1:
                            after_dve(("XR", g, lev - 1))
                        four_products(f, lambda i: r_inv[:, g, i, :], lambda i: xb[:, g, i, :])
                    elif what == "XR":
                        after_act(("X", g, lev))
                        if lev > 1:
                            after_dve(("XR", g, lev - 1))
                        four_products(f, lambda i: xb[:, g, i, :], lambda i: r_inv[:, g, i, :])
                    elif what == "W":
                        after_dve(("XR", g, LEVELS - 1))
                        after_pool(("kbg", g))
                        four_products(f, lambda i: kbg[:, g, i, :], lambda i: r_inv[:, g, i, :])
                    elif what == "U":
                        four_products(f, lambda i: r_inv[:, g, i, :], lambda i: vb[:, g, i, :])

                after_act(("W", 1, 0))
                after_dve(("U", 1, 0))

                def turn(i, c):
                    n = FOX_CHUNK[(i, c)]
                    if n >= 1:
                        pe.wait_ge(*((pt_act, j * (NFC // 2) + (n - 1) // 2 + 1) if n % 2 == 1 else (pt_dve, j * (NFC // 2) + n // 2)))
                    for kb in range(4 * c, min(4 * c + 4, FOX_TILES[i][1] + 1)):
                        last = nc.tensor.transpose(fox_t[:, (kb - 4 * c) * P:(kb - 4 * c + 1) * P], probs[i % 2][:, kb * P:(kb + 1) * P], ident)
                    last.then_inc(fox_turned, 1)

                def times_v(i, c):
                    n, (hh, qb) = FOX_CHUNK[(i, c)], FOX_TILES[i]
                    pe.wait_ge(*((pt_act, j * (NFC // 2) + n // 2 + 1) if n % 2 == 0 else (pt_dve, j * (NFC // 2) + n // 2 + 1)))
                    if c == 0:
                        pe.wait_ge(fox_read, j * NFT + i + 1)
                    for kb in range(4 * c, min(4 * c + 4, qb + 1)):
                        last = nc.tensor.matmul(fox_o[:, 0:FOX_DIM], probs_t[n % 2][:, kb - 4 * c, :], v_tok[:, kb, hh * FOX_DIM:(hh + 1) * FOX_DIM],
                                                start=(kb == 0), stop=(kb == qb))
                    last.then_inc(fox_pv, 1)

                def beside_scan(i, n):
                    if with_gemm and i < NCHUNK:
                        unit_index, k = divmod(SCAN_STEP_PARTS * i + n, KT)
                        part(SCAN_UNITS[unit_index], j + 1, k)

                for i in range(NCHUNK + 1):
                    if i < NCHUNK:
                        half = 64 * (i % 2)
                        rows, (g, tt) = slice(half, half + 64), divmod(i // 2, 4)
                        toks = slice(half, half + 64)
                        pe.wait_ge(state_ready, j * (NCHUNK + 1) + i + 1)
                        nc.tensor.matmul(scan_a[rows, 0:P], t_inv[:, g, tt, toks], state[:, :], start=True, stop=True).then_inc(scan_v, 1)
                        if i >= 2:
                            pe.wait_ge(o_read, j * NCHUNK + i - 1)
                        nc.tensor.matmul(scan_b[rows, 0:P], qdT[:, i // 2, toks], state[:, :], start=True, stop=False)
                        hh, qb = FOX_TILES[i]
                        pe.wait_ge(q_ready, j * NFT + i + 1)
                        if i == 0:
                            pe.wait_ge(k_lo_ready, j * 4 + 4)
                        else:
                            pe.wait_ge(fox_max, j * NFT + i + 1)
                        nk = (qb + 1) * P
                        for c in range(0, nk, 512):
                            ce = min(c + 512, nk)
                            nc.tensor.matmul(fox_s[:, c:ce], q_hi[i % 2][:, :], k_split[hh][:, c:ce], start=True, stop=False)
                            nc.tensor.matmul(fox_s[:, c:ce], q_lo[i % 2][:, :], k_split[hh][:, c:ce], start=False, stop=True)
                        nc.tensor.matmul(fox_s[:, qb * P:nk], ident_bf[:, :], causal_bf[:, :], start=False, stop=True,
                                         skip_group_check=True).then_inc(fox_scored, 1)
                    beside_scan(i, 0)
                    if i >= 1:
                        pe.wait_ge(fox_exp, j * NFT + i)
                        turn(i - 1, 0)
                    if i < NCHUNK:
                        pe.wait_ge(v_new_ready, j * NCHUNK + i + 1)
                        nc.tensor.matmul(scan_a[:, P:2 * P], kd[rows, i // 2, :], v_new[rows, :], start=True, stop=True).then_inc(scan_s, 1)
                        nc.tensor.matmul(scan_b[rows, 0:P], a_t[rows, i // 2, toks], v_new[rows, :], start=False, stop=True).then_inc(scan_o, 1)
                    beside_scan(i, 1)
                    if i >= 1:
                        if FOX_TILES[i - 1][1] >= 4:
                            turn(i - 1, 1)
                        times_v(i - 1, 0)
                        if FOX_TILES[i - 1][1] >= 4:
                            times_v(i - 1, 1)
                    beside_scan(i, 2)

            with pe.Fori(0, GDN_HEADS - 1) as j:
                head(j, True)
            head(GDN_HEADS - 1, False)
            head_loop_over(pe)
            pe.wait_ge(w_lo_ready, W_OUT_SPLIT)

            def turn_mixed(t):
                pe.wait_ge(w_loaded[t % 2], 16 * (SLOT_LOADS[t % 2] - NT // 2 + t // 2 + 1))
                if t >= 2:
                    pe.wait_ge(m_lo_ready, t)
                for k in range(KT):
                    last = nc.tensor.transpose(mixed_banks(t)[:, k * P:(k + 1) * P], w_raw[t % 2][:, k, :], ident)
                last.then_inc(m_turned, 1)

            def turn_h2(t):
                pe.wait_ge(h2_normed, t + 1)
                if t >= 1:
                    pe.wait_ge(h2_lo_ready, t)
                for k in range(KT):
                    last = nc.tensor.transpose(banks(6, 2)[:, k * P:(k + 1) * P], y_buf[t % 2][:, k * P:(k + 1) * P], ident)
                last.then_inc(h2_turned, 1)

            turn_mixed(0)
            for t in range(NT):
                if t + 1 < NT:
                    turn_mixed(t + 1)
                pe.wait_ge(m_lo_ready, t + 1)
                if t >= 2:
                    pe.wait_ge(y_done, t - 1)
                for n in range(2):
                    acc = banks(2 * (t % 2) + n)
                    cols = slice(n * HALF, (n + 1) * HALF)
                    for k in range(KT):
                        nc.tensor.matmul(acc, m_hi[t % 2][:, k, :], big_hi[:, k, cols], start=(k == 0), stop=False)
                        nc.tensor.matmul(acc, m_hi[t % 2][:, k, :], big_lo[:, k, cols], start=False, stop=False)
                        last = nc.tensor.matmul(acc, m_lo[t % 2][:, k, :], big_hi[:, k, cols], start=False, stop=(k == KT - 1))
                last.then_inc(out_done, 1)
                if t >= 1:
                    turn_h2(t - 1)

            def up(h, f, s, wait):
                pe.wait_ge(mlp_lo, f + (h * STEPS + 1))
                if wait:
                    pe.wait_ge(relu_done, f + (h * FT - 1))
                toks = slice(h * HALF, (h + 1) * HALF)
                for k in range(KT):
                    nc.tensor.matmul(banks(s), u_hi[s][:, k, :], h2_hi[:, k, toks], start=(k == 0), stop=False)
                    nc.tensor.matmul(banks(s), u_hi[s][:, k, :], h2_lo[:, k, toks], start=False, stop=False)
                    last = nc.tensor.matmul(banks(s), u_lo[s][:, k, :], h2_hi[:, k, toks], start=False, stop=(k == KT - 1))
                last.then_inc(mlp_done, 1)

            def down(h, f, s, first, final_step):
                pe.wait_ge(act_lo, f + (h * FT + 1))
                for m in (*range(2, KT), 0, 1):
                    if first and m == 1:
                        pe.wait_ge(relu_done, (h + 1) * FT)
                    nc.tensor.matmul(banks(m), u_hi[s][:, m, :], a_hi[s][:, :], start=first, stop=False)
                    nc.tensor.matmul(banks(m), u_hi[s][:, m, :], a_lo[s][:, :], start=False, stop=False)
                    last = nc.tensor.matmul(banks(m), u_lo[s][:, m, :], a_hi[s][:, :], start=False, stop=final_step)
                last.then_inc(mlp_done, 1)

            def turn_final(h, tts):
                pe.wait_ge(down_act, (h + 1) * KT // 2)
                pe.wait_ge(down_dve, (h + 1) * KT // 2)
                for tt in tts:
                    if tt >= 3:
                        pe.wait_ge(final_step, h * HT + tt - 2)
                    for m in range(KT):
                        last = nc.tensor.transpose(final_banks(tt)[:, m * P:(m + 1) * P], down_T[:, m, tt * P:(tt + 1) * P], ident)
                    last.then_inc(final_turned, 1)

            for h in range(2):
                if h == 0:
                    pe.wait_ge(h2_lo_ready, HT)
                    pe.wait_ge(y_done, NT - 1)
                else:
                    pe.wait_ge(h2_lo_ready, NT)
                    pe.wait_ge(down_act, 1)
                up(h, 0, 0, False)
                if h == 1:
                    pe.wait_ge(down_dve, 1)
                up(h, 1, 1, False)
                if h == 0:
                    turn_h2(NT - 1)
                else:
                    turn_final(0, range(0, 3))
                up(h, 2, 0, True)
                up(h, 3, 1, True)
                if h == 1:
                    turn_final(0, range(3, HT))
                with pe.Fori(2, FT // 2) as i:
                    up(h, i * 2, 0, True)
                    up(h, i * 2 + 1, 1, True)
                pe.wait_ge(relu_done, (h + 1) * FT - 1)
                if h == 1:
                    pe.wait_ge(final_step, HT)
                down(h, 0, 0, True, False)
                down(h, 1, 1, False, False)
                with pe.Fori(1, FT // 2 - 1) as i:
                    down(h, i * 2, 0, False, False)
                    down(h, i * 2 + 1, 1, False, False)
                down(h, FT - 2, 0, False, False)
                down(h, FT - 1, 1, False, True)
            turn_final(1, range(HT))


_INS = ['x', 'pre_mix_norm', 'w_in', 'fox_f_bias', 'fox_out_norm', 'gdn_conv_w', 'gdn_a_log', 'gdn_dt_bias', 'gdn_out_norm',
        'w_out', 'post_mix_norm', 'pre_mlp_norm', 'w_up', 'w_down', 'post_mlp_norm']
_OUTS = [((1, SEQ, D), 'float32')]


def shape_constants():
    import numpy as np
    row, col = np.arange(P)[:, None], np.arange(P)[None, :]
    tiles = np.zeros((N_CONST + 1, P, P), np.float32)
    tiles[IDENT] = row == col
    same_chunk = row // CHUNK == col // CHUNK
    tiles[DECAY_MASK] = np.where(same_chunk & (col >= row), 0.0, -1e30)
    tiles[N_CONST] = np.where(col <= row, 0.0, -1e30)
    for lev in range(LEVELS):
        size = 2 ** lev
        tiles[LEVEL_MASK + lev] = (row // (2 * size) == col // (2 * size)) & (col // size % 2 == 1) & (row // size % 2 == 0)
    keep = np.ones((P, SEQ), np.float32)
    keep[ROW_G:ROW_G + 32, ::CHUNK] = 0.0
    return np.ascontiguousarray(tiles.transpose(1, 0, 2).reshape(P, (N_CONST + 1) * P)), keep


def kernel(**inputs):
    import numpy as _np
    import concourse.bacc as _bacc
    from concourse import mybir as _mybir
    from concourse.bass_utils import run_bass_kernel_spmd as _run

    nc = _bacc.Bacc("TRN2", target_bir_lowering=False, num_devices=1)
    given = {name: _np.ascontiguousarray(inputs[name]) for name in _INS}
    given["const_tiles"], given["scan_keep"] = shape_constants()
    arrays, args = {}, []
    for name, a in given.items():
        arrays[f"in_{name}_dram"] = a
        args.append(nc.dram_tensor(f"in_{name}_dram", a.shape, _mybir.dt.from_np(a.dtype), kind="ExternalInput").ap())
    for i, (shape, dtype) in enumerate(_OUTS):
        dt = _mybir.dt.from_np(_np.dtype(dtype))
        args.append(nc.dram_tensor(f"out_{i}_dram", shape, dt, kind="ExternalOutput").ap())
    args.append(nc.dram_tensor("mixed", (SEQ, P + D), F32, kind="Internal").ap())
    args.append(nc.dram_tensor("gate_dram", (FOX_HEADS + GDN_HEADS, SEQ), F32, kind="Internal").ap())
    build(nc, *args)
    r = _run(nc, [arrays], core_ids=[0])
    got = tuple(r.results[0][f"out_{i}_dram"] for i in range(len(_OUTS)))
    return got[0]
```
